# Optimizing a Trainium2 kernel written in Bass

```python
import jax, jax.numpy as jnp
from jax import lax
import numpy as np

'''One inference step of a hybrid decoder layer stack (Hymba-style parallel head groups).

Each layer: RMSNorm -> one combined input projection whose columns are split between
  group A: multi-scale retention (RetNet, chunkwise recurrent form, rotary xPos-style phases), 4 heads
  group B: MoBA block-sparse softmax attention (NoPE), 8 heads, blocks of 256, top-3 past blocks + own block
-> concatenated head-group outputs -> one output projection -> residual add
-> RMSNorm -> top-4-of-32 clamped-SwiGLU experts (gpt-oss router with bias) -> residual add.
Final RMSNorm.

Inputs:
  x_prompt (BATCH, SEQ, D_MODEL), x_sample (DEC_BATCH, DEC_SEQ, D_MODEL)
  cache_k, cache_v (DEPTH, N_PHYS, PAGE_SIZE, MOBA_HEADS, MOBA_HD)  paged MoBA K/V pool
  state_ret (DEPTH, DEC_BATCH, RET_HEADS, RET_DK, RET_DV)          retention recurrent state
  page_table (DEC_BATCH, N_PAGES) int32, then the layer weights.
Returns tuple:
  y_prompt (BATCH, SEQ, D_MODEL), y_sample (DEC_BATCH, DEC_SEQ, D_MODEL),
  k_prompt, v_prompt (DEPTH, BATCH, SEQ, MOBA_HEADS, MOBA_HD),
  ret_state_prompt (DEPTH, BATCH, RET_HEADS, RET_DK, RET_DV),
  k_sample, v_sample (DEPTH, DEC_BATCH, DEC_SEQ, MOBA_HEADS, MOBA_HD),
  ret_state_sample (DEPTH, DEC_BATCH, RET_HEADS, RET_DK, RET_DV).
'''

D_MODEL = 1024
BATCH = 1
SEQ = 256
DEPTH = 1
DEC_BATCH = 8
DEC_SEQ = 4
PAST_LEN = 2048
PAGE_SIZE = 128

D_MIX = D_MODEL
D_RET = D_MIX // 2
D_MOBA = D_MIX - D_RET
RET_HEADS = 4
RET_DK = D_RET // RET_HEADS
RET_DV = D_RET // RET_HEADS
RET_CHUNK = 128
MOBA_HEADS = 8
MOBA_HD = D_MOBA // MOBA_HEADS
MOBA_BLOCK = 256
MOBA_TOPK = 3
MOBA_Q_BLOCK = 64
N_EXPERTS = 32
TOP_K = 4
D_FF = D_MODEL
SWIGLU_LIMIT = 7.0
SWIGLU_ALPHA = 1.702
ROPE_BASE = 10000.0
EPS = 1e-5
D_IN = 4 * D_RET + 3 * D_MOBA
SPLIT_POINTS = (D_RET, 2 * D_RET, 3 * D_RET, 4 * D_RET, 4 * D_RET + D_MOBA, 4 * D_RET + 2 * D_MOBA)
NEG = -1e30

kernel_name = 'hymba_retention_moba_moe_step'

def rmsnorm(x, g):
    xf = x.astype(jnp.float32)
    return xf * lax.rsqrt(jnp.mean(jnp.square(xf), axis=-1, keepdims=True) + EPS) * g

def rotary(x, pos):
    half = x.shape[-1] // 2
    inv = ROPE_BASE ** (-jnp.arange(half, dtype=jnp.float32) / half)
    ang = pos.astype(jnp.float32)[:, None] * inv[None, :]
    c = jnp.cos(ang)[:, None, :]
    s = jnp.sin(ang)[:, None, :]
    x1, x2 = x[..., :half], x[..., half:]
    return jnp.concatenate([x1 * c - x2 * s, x1 * s + x2 * c], axis=-1)

def project(x, norm_g, w_in, pos):
    b, l, _ = x.shape
    z = jnp.einsum('bld,de->ble', rmsnorm(x, norm_g), w_in).astype(jnp.float32)
    rq, rk, rv, rg, mq, mk, mv = jnp.split(z, SPLIT_POINTS, axis=-1)
    rq = rotary(rq.reshape(b, l, RET_HEADS, RET_DK), pos)
    rk = rotary(rk.reshape(b, l, RET_HEADS, RET_DK), pos) * RET_DK ** -0.5
    rv = rv.reshape(b, l, RET_HEADS, RET_DV)
    mq = mq.reshape(b, l, MOBA_HEADS, MOBA_HD)
    mk = mk.reshape(b, l, MOBA_HEADS, MOBA_HD)
    mv = mv.reshape(b, l, MOBA_HEADS, MOBA_HD)
    return rq, rk, rv, rg, mq, mk, mv

def retention_chunked(q, k, v, s0, chunk):
    b, l, h, dk = q.shape
    dv = v.shape[-1]
    nc = l // chunk
    log_g = jnp.log1p(-jnp.exp2(-5.0 - jnp.arange(h, dtype=jnp.float32)))
    n = jnp.arange(chunk, dtype=jnp.float32)
    rel = n[:, None] - n[None, :]
    causal = rel >= 0
    decay_in = jnp.where(causal[None], jnp.exp(jnp.where(causal, rel, 0.0)[None] * log_g[:, None, None]), 0.0)
    q_dec = jnp.exp((n[:, None] + 1.0) * log_g[None, :])
    k_dec = jnp.exp((chunk - 1.0 - n[:, None]) * log_g[None, :])
    chunk_dec = jnp.exp(chunk * log_g)

    def to_chunks(t):
        return t.reshape(b, nc, chunk, h, t.shape[-1]).swapaxes(0, 1)

    def step(s, xs):
        qc, kc, vc = xs
        scores = jnp.einsum('bnhd,bmhd->bhnm', qc, kc) * decay_in[None]
        inner = jnp.einsum('bhnm,bmhv->bnhv', scores, vc)
        cross = jnp.einsum('bnhd,bhdv->bnhv', qc * q_dec[None, :, :, None], s)
        s_new = chunk_dec[None, :, None, None] * s + jnp.einsum('bmhd,bmhv->bhdv', kc * k_dec[None, :, :, None], vc)
        return s_new, inner + cross

    s_final, o = lax.scan(step, s0, (to_chunks(q), to_chunks(k), to_chunks(v)))
    return o.swapaxes(0, 1).reshape(b, l, h, dv), s_final

def moba_attend_seq(q, k_all, v_all, q_pos):
    l, h, hd = q.shape
    t = k_all.shape[0]
    nb = -(-t // MOBA_BLOCK)
    pad = nb * MOBA_BLOCK - t
    kb = jnp.pad(k_all, ((0, pad), (0, 0), (0, 0))).reshape(nb, MOBA_BLOCK, h, hd).transpose(2, 0, 1, 3)
    vb = jnp.pad(v_all, ((0, pad), (0, 0), (0, 0))).reshape(nb, MOBA_BLOCK, h, hd).transpose(2, 0, 1, 3)
    k_mean = jnp.mean(kb.astype(jnp.float32), axis=2)
    k_sel = min(MOBA_TOPK, nb)
    qb = MOBA_Q_BLOCK if l % MOBA_Q_BLOCK == 0 else l
    blk_ids = jnp.arange(nb)
    offs = jnp.arange(MOBA_BLOCK)
    h_idx = jnp.arange(h)[None, :, None]
    scale = hd ** -0.5

    def one_block(args):
        qblk, pblk = args
        qf = qblk.astype(jnp.float32)
        cur = pblk // MOBA_BLOCK
        past = blk_ids[None, :] < cur[:, None]
        gate = jnp.einsum('qhd,hnd->qhn', qf, k_mean)
        gate = jnp.where(past[:, None, :], gate, NEG)
        _, top_i = lax.top_k(gate, k_sel)
        top_ok = jnp.take_along_axis(jnp.broadcast_to(past[:, None, :], gate.shape), top_i, axis=-1)
        idx = jnp.concatenate([top_i, jnp.broadcast_to(cur[:, None, None], (qb, h, 1))], axis=-1)
        ok = jnp.concatenate([top_ok, jnp.ones((qb, h, 1), dtype=bool)], axis=-1)
        kg = kb[h_idx, idx].astype(jnp.float32)
        vg = vb[h_idx, idx].astype(jnp.float32)
        key_pos = idx[..., None] * MOBA_BLOCK + offs
        mask = ok[..., None] & (key_pos <= pblk[:, None, None, None])
        s = jnp.einsum('qhd,qhjkd->qhjk', qf, kg) * scale
        s = jnp.where(mask, s, -jnp.inf)
        p = jax.nn.softmax(s.reshape(qb, h, -1), axis=-1).reshape(s.shape)
        return jnp.einsum('qhjk,qhjkd->qhd', p, vg)

    out = lax.map(one_block, (q.reshape(l // qb, qb, h, hd), q_pos.reshape(l // qb, qb)))
    return out.reshape(l, h, hd)

def moe(h, router_w, router_b, w_gu, b_gu, w_d, b_d):
    tok = h.reshape(-1, D_MODEL).astype(jnp.float32)
    logits = tok @ router_w + router_b
    top_v, top_i = lax.top_k(logits, TOP_K)
    top_w = jax.nn.softmax(top_v, axis=-1)
    gates = jnp.einsum('tk,tke->te', top_w, jax.nn.one_hot(top_i, N_EXPERTS, dtype=jnp.float32))

    def expert(acc, xs):
        wgu, bgu, wd, bd, g = xs
        u = tok @ wgu + bgu
        glu = jnp.minimum(u[:, ::2], SWIGLU_LIMIT)
        lin = jnp.clip(u[:, 1::2], -SWIGLU_LIMIT, SWIGLU_LIMIT)
        a = glu * jax.nn.sigmoid(SWIGLU_ALPHA * glu) * (lin + 1.0)
        return acc + g[:, None] * (a @ wd + bd), None

    acc, _ = lax.scan(expert, jnp.zeros_like(tok), (w_gu, b_gu, w_d, b_d, gates.T))
    return acc

def merge_and_channel_mix(x, rg, ret_o, moba_o, ret_norm_g, w_out, norm2_g, router_w, router_b, w_gu, b_gu, w_d, b_d):
    b, l, _ = x.shape
    mu = jnp.mean(ret_o, axis=-1, keepdims=True)
    var = jnp.mean(jnp.square(ret_o - mu), axis=-1, keepdims=True)
    ret = ((ret_o - mu) * lax.rsqrt(var + EPS)).reshape(b, l, D_RET) * ret_norm_g * jax.nn.silu(rg)
    mix = jnp.concatenate([ret, moba_o.reshape(b, l, D_MOBA)], axis=-1)
    hres = x.astype(jnp.float32) + jnp.einsum('ble,ed->bld', mix, w_out)
    return hres + moe(rmsnorm(hres, norm2_g), router_w, router_b, w_gu, b_gu, w_d, b_d).reshape(b, l, D_MODEL)

def setup_inputs(seed: int = 0) -> dict:
    key = jax.random.key(seed)
    ks = jax.random.split(key, 18)
    f32 = jnp.float32
    n_pages = PAST_LEN // PAGE_SIZE
    n_used = DEC_BATCH * n_pages
    n_phys = n_used + n_used // 4

    def nrm(k, shape, s):
        return jax.random.normal(k, shape, f32) * s

    return {
        'x_prompt': nrm(ks[0], (BATCH, SEQ, D_MODEL), 1.0),
        'x_sample': nrm(ks[1], (DEC_BATCH, DEC_SEQ, D_MODEL), 1.0),
        'cache_k': nrm(ks[2], (DEPTH, n_phys, PAGE_SIZE, MOBA_HEADS, MOBA_HD), 1.0),
        'cache_v': nrm(ks[3], (DEPTH, n_phys, PAGE_SIZE, MOBA_HEADS, MOBA_HD), 1.0),
        'state_ret': nrm(ks[4], (DEPTH, DEC_BATCH, RET_HEADS, RET_DK, RET_DV), 0.3),
        'page_table': jax.random.permutation(ks[5], n_phys)[:n_used].reshape(DEC_BATCH, n_pages).astype(jnp.int32),
        'norm1_g': 1.0 + nrm(ks[6], (DEPTH, D_MODEL), 0.02),
        'w_in': nrm(ks[7], (DEPTH, D_MODEL, D_IN), D_MODEL ** -0.5),
        'ret_norm_g': 1.0 + nrm(ks[8], (DEPTH, D_RET), 0.02),
        'w_out': nrm(ks[9], (DEPTH, D_MIX, D_MODEL), D_MIX ** -0.5),
        'norm2_g': 1.0 + nrm(ks[10], (DEPTH, D_MODEL), 0.02),
        'router_w': nrm(ks[11], (DEPTH, D_MODEL, N_EXPERTS), D_MODEL ** -0.5),
        'router_b': nrm(ks[12], (DEPTH, N_EXPERTS), 0.01),
        'w_gate_up': nrm(ks[13], (DEPTH, N_EXPERTS, D_MODEL, 2 * D_FF), D_MODEL ** -0.5),
        'b_gate_up': nrm(ks[14], (DEPTH, N_EXPERTS, 2 * D_FF), 0.01),
        'w_down': nrm(ks[15], (DEPTH, N_EXPERTS, D_FF, D_MODEL), D_FF ** -0.5),
        'b_down': nrm(ks[16], (DEPTH, N_EXPERTS, D_MODEL), 0.01),
        'final_norm_g': 1.0 + nrm(ks[17], (D_MODEL,), 0.02),
    }

def reference(x_prompt, x_sample, cache_k, cache_v, state_ret, page_table, norm1_g, w_in, ret_norm_g, w_out, norm2_g, router_w, router_b, w_gate_up, b_gate_up, w_down, b_down, final_norm_g):
    bp, lp, _ = x_prompt.shape
    bs, ls, _ = x_sample.shape
    past_len = page_table.shape[1] * PAGE_SIZE
    pos_p = jnp.arange(lp, dtype=jnp.int32)
    pos_s = past_len + jnp.arange(ls, dtype=jnp.int32)
    chunk_s = RET_CHUNK if ls % RET_CHUNK == 0 else ls
    yp, ys = x_prompt, x_sample
    kp_l, vp_l, sp_l, ks_l, vs_l, ss_l = [], [], [], [], [], []
    for layer in range(DEPTH):
        ffn_args = (ret_norm_g[layer], w_out[layer], norm2_g[layer], router_w[layer], router_b[layer],
                    w_gate_up[layer], b_gate_up[layer], w_down[layer], b_down[layer])
        rq, rk, rv, rg, mq, mk, mv = project(yp, norm1_g[layer], w_in[layer], pos_p)
        ret_o, s_p = retention_chunked(rq, rk, rv, jnp.zeros((bp, RET_HEADS, RET_DK, RET_DV), jnp.float32), RET_CHUNK)
        moba_o = lax.map(lambda a: moba_attend_seq(a[0], a[1], a[2], pos_p), (mq, mk, mv))
        yp = merge_and_channel_mix(yp, rg, ret_o, moba_o, *ffn_args)
        kp_l.append(mk)
        vp_l.append(mv)
        sp_l.append(s_p)
        rq, rk, rv, rg, mq, mk, mv = project(ys, norm1_g[layer], w_in[layer], pos_s)
        ret_o, s_s = retention_chunked(rq, rk, rv, state_ret[layer].astype(jnp.float32), chunk_s)
        ck = cache_k[layer]
        cv = cache_v[layer]

        def sample_seq(a, ck=ck, cv=cv):
            q, kn, vn, pages = a
            k_past = ck[pages].reshape(past_len, MOBA_HEADS, MOBA_HD).astype(jnp.float32)
            v_past = cv[pages].reshape(past_len, MOBA_HEADS, MOBA_HD).astype(jnp.float32)
            k_all = jnp.concatenate([k_past, kn], axis=0)
            v_all = jnp.concatenate([v_past, vn], axis=0)
            return moba_attend_seq(q, k_all, v_all, pos_s)

        moba_o = lax.map(sample_seq, (mq, mk, mv, page_table))
        ys = merge_and_channel_mix(ys, rg, ret_o, moba_o, *ffn_args)
        ks_l.append(mk)
        vs_l.append(mv)
        ss_l.append(s_s)
    y_prompt = rmsnorm(yp, final_norm_g)
    y_sample = rmsnorm(ys, final_norm_g)
    k_prompt = jnp.stack(kp_l)
    v_prompt = jnp.stack(vp_l)
    ret_state_prompt = jnp.stack(sp_l)
    k_sample = jnp.stack(ks_l)
    v_sample = jnp.stack(vs_l)
    ret_state_sample = jnp.stack(ss_l)
    return (y_prompt, y_sample, k_prompt, v_prompt, ret_state_prompt, k_sample, v_sample, ret_state_sample)


_drawn_inputs = setup_inputs


def setup_inputs(seed=0):
    import zlib

    import numpy as np

    out = dict(_drawn_inputs(seed))
    spreads = {}
    factors = {'b_gate_up': 8.0, 'b_down': 8.0, 'final_norm_g': 2.853}
    for name, (base, spread) in spreads.items():
        noise = np.random.default_rng([zlib.crc32(name.encode()), seed]).standard_normal(out[name].shape)
        drawn = base * np.exp(spread * noise) if base else spread * noise
        out[name] = __import__('jax').numpy.asarray(drawn.astype(out[name].dtype))
    for name, factor in factors.items():
        out[name] = (out[name] * factor).astype(out[name].dtype)
    return out
```

```python
from contextlib import ExitStack

import numpy as np

import concourse.bass as bass
from concourse import mybir

F32 = mybir.dt.float32
I32 = mybir.dt.int32
U32 = mybir.dt.uint32
ALU = mybir.AluOpType
ACT = mybir.ActivationFunctionType
AXX = mybir.AxisListType.X

P = 128
D = 1024
KC = D // P
LP = 256
NS = 32
SEQS = 8
PAGES = 16
TILES = 3
TOK = LP + NS
COLS = (P, P, NS)
E = 32
F2 = 2048
SLOTS = 64
PAIRS = E // 2
ROUNDS = -(-TOK // SLOTS)
EXTRA = 18
BIG = 1.0e4
NEG = -1.0e30
EPS = 1e-5
RH = 4
MH = 8
SCALE = 64 ** -0.5
KSCALE = 128 ** -0.5
LIMIT = 7.0
ALPHA = 1.702
HEADS0 = (0, 2, 4, 6, 1, 3, 5, 7)
HEADS1 = (0, 2, 1, 3, 4, 6, 5, 7)
GAMMA = [1.0 - 2.0 ** (-5 - h) for h in range(RH)]


def shape_constants():
    parts = []

    def put(name, a):
        full = np.zeros((P, a.shape[1]), np.float32)
        full[: a.shape[0]] = a
        parts.append((name, full))

    put("ident", np.eye(P))
    half = 64
    inv = (np.float32(10000.0) ** (-np.arange(half, dtype=np.float32) / half)).astype(np.float32)
    pos = [np.arange(P), P + np.arange(P), PAGES * P + np.arange(NS) % 4]
    ang = [(p.astype(np.float32)[:, None] * inv[None]).astype(np.float32) for p in pos]
    for name, f in (("cos", np.cos), ("sin", np.sin)):
        t = np.zeros((P, TILES * half), np.float32)
        for n, a in enumerate(ang):
            t[: len(a), n * half:(n + 1) * half] = f(a.astype(np.float64))
        put(name, t)
    lg = np.log1p(-np.exp2(-5.0 - np.arange(RH)))
    n = np.arange(P)
    rel = n[None, :] - n[:, None]
    decay = [np.where(rel >= 0, np.exp(np.maximum(rel, 0) * g), 0.0) * KSCALE for g in lg]
    put("decay", np.concatenate(decay, 1))
    seq, step = np.arange(NS) // 4, np.arange(NS) % 4
    same = seq[:, None] == seq[None, :]
    srel = step[None, :] - step[:, None]
    put("decay_s", np.concatenate(
        [np.where(same & (srel >= 0), np.exp(np.maximum(srel, 0) * g), 0.0) * KSCALE for g in lg], 1))
    qd = np.zeros((P, TILES * RH))
    kd = np.zeros((P, TILES * RH))
    for t in range(TILES):
        m, chunk = (n, P) if t < 2 else (step, 4)
        qd[: len(m), t * RH:(t + 1) * RH] = np.exp((m[:, None] + 1.0) * lg)
        kd[: len(m), t * RH:(t + 1) * RH] = np.exp((chunk - 1.0 - m[:, None]) * lg) * KSCALE
    put("q_dec", qd)
    put("k_dec", kd)
    put("causal", np.where(n[None, :] <= n[:, None], 0.0, NEG))
    own = np.full((P, 2, NS), NEG)
    for g in range(2):
        for r in range(P):
            s, i = 4 * g + r // 32, r % 4
            own[r, g, 4 * s:4 * s + i + 1] = 0.0
    put("own_mask", own.reshape(P, -1))
    put("seq_mask", (seq[:, None] == np.arange(SEQS)[None]) * 1.0)
    valid = np.ones((P, TILES))
    valid[NS:, 2] = 0.0
    put("before8", np.tile(np.tril(np.ones((8, 8)), -1).reshape(1, 64), (P, 1)))
    put("valid", valid)
    put("eps", np.full((P, 1), EPS))
    first_late = sum(a.shape[1] for _, a in parts)
    put("iota", np.tile(np.arange(ROUNDS * SLOTS, dtype=np.float32), (P, 1)))
    put("earlier", np.triu(np.ones((P, P)), 1))
    put("ones", np.ones((P, P)))
    table, at = {"late": (first_late, 0)}, 0
    for name, a in parts:
        table[name] = (at, a.shape[1])
        at += a.shape[1]
    return table, np.ascontiguousarray(np.concatenate([a for _, a in parts], 1))


class Ring:

    def __init__(self, banks, full, empty):
        self.banks, self.full, self.empty, self.n, self.base = banks, full, empty, 0, 0

    def bank(self):
        return self.banks[self.n % 2]

    def wait_empty(self, pe):
        if self.n >= 2:
            pe.wait_ge(self.empty, self.base + (self.n - 1))

    def filled(self, instruction):
        instruction.then_inc(self.full, 1)
        self.n += 1
        return self.n

    def wait_full(self, eng):
        eng.wait_ge(self.full, self.base + (self.n + 1))

    def emptied(self, instruction):
        instruction.then_inc(self.empty, 1)
        self.n += 1
        return self.n

    def loop(self, base):
        self.base = base

    def leave(self, passes, per_pass):
        self.base = 0
        self.n += (passes - 1) * per_pass


def build_kernel(nc, t, table, outs):
    with ExitStack() as ctx:
        def sem(name):
            return ctx.enter_context(nc.semaphore(name))

        ncols = table["late"][0]
        late_cols = sum(c for _, c in table.values()) - ncols
        WORDS = 53176
        arena = ctx.enter_context(nc.sbuf_tensor("arena", [P, WORDS], F32))
        psum = ctx.enter_context(nc.psum_tensor("psum", [P, 8, 512], F32))

        def at(start, *dims):
            flat = arena[:, start:start + int(np.prod(dims))]
            if len(dims) == 1:
                return flat
            names = "abcd"[:len(dims)]
            return flat.rearrange(f"p ({' '.join(names)}) -> p {' '.join(names)}",
                                  **dict(zip(names, dims)))

        gu = at(0, KC, F2)
        win = at(0, 3, KC, 512)
        state = at(12288, SEQS, RH, P)
        DN = 16384
        dn = at(DN, KC, D)
        kt_sb = at(DN, 2, 4, 4, P)
        x_sb = at(DN + 4096, TILES, D)
        pt_prompt = at(DN, 24, P)
        s_prompt = at(DN + 4096, 24, P)
        rot_q = at(DN, TILES, RH, P)
        rot_k = at(DN + 1536, TILES, RH, P)
        rq_t = at(DN + 3072, RH, TOK)
        rk_t = at(DN + 4224, RH, TOK)
        k_dec = at(DN + 5376, TILES, RH, P)
        q_dec = at(DN + 6912, 2, RH, P)
        ret_o, sig_g = rot_q, rot_k

        C0 = DN + 8192
        consts = at(C0, ncols)

        def const(name):
            a, n = table[name]
            return consts[:, a:a + n]

        ident = const("ident")
        cur = C0 + ncols
        gain = at(cur, 20); cur += 20
        gain_in = at(cur, P); cur += P
        stat = at(cur, 64); cur += 64
        own_s = at(cur, 2, NS); cur += 2 * NS
        sm = at(cur, 2, 64); cur += 128
        pm = at(cur, 64); cur += 64
        page_sb = at(cur, SEQS * PAGES)[0:1].bitcast(I32); cur += SEQS * PAGES
        cmp = at(cur, 2, 8, 8); cur += 128
        KV = cur; cur += 8192
        kv = at(KV, 4, 4, 512)
        HT = cur; cur += 2304
        h_t = at(HT, KC, TOK)
        Z = cur; cur += 4608
        z = at(Z, 3, TILES, 512)
        mv_s = at(cur, 512); cur += 512
        SR = cur; cur += 4096
        s_raw = at(SR, 2, PAGES * P)
        Q = cur; cur += 3328
        mq_t = at(Q, 4, TOK)
        mk_t = at(Q + 1152, 4, TOK)
        q_blk = at(Q + 2304, SEQS, 4, NS)
        MX = cur; cur += 2304
        mix_t = at(MX, KC, TOK)
        o_sb = (at(SR + 1024, 512), mv_s)
        pt_sb = at(cur, 2, 512); cur += 1024
        pt_own = at(DN + 7936, 2, P)
        assert cur <= WORDS, cur
        tmp = at(Q, TILES, RH, P)
        sc_p = at(Q + 1536, 2, RH, P)
        st1 = at(Q + 2560, RH, P)
        sc_s = at(Q + 3072, RH, NS)
        qdm = at(HT, RH, SEQS, 36)
        qdm_flat = at(HT, RH, 288)
        qd_t = at(HT + 1152, RH, P)
        st2 = at(HT + 1664, RH, P)
        v_blk = at(SR, SEQS, P)
        y = at(SR, TILES, D)
        f_gain = at(SR + 3072, D)
        h2_t = at(HT, KC, TOK)
        hn = at(Z, TILES, D)
        out2 = at(Z + 3072, D)
        xt = at(KV, KC, P)
        x_nat = at(KV + 1024, D)
        g_sb = at(KV + 2048, 512)
        l_sb = at(KV + 2560, 512)
        sg_sb = at(KV + 3072, 512)
        a_sb = at(KV + 3584, 512)
        at_sb = at(KV + 4096, 4, P)
        sel = at(KV + 4608, TILES, 2, SLOTS)
        selg = at(KV + 4992, TILES, 2, SLOTS)
        sgt = at(KV + 5376, TILES * P)
        esel = at(KV + 5760, 2, SLOTS)
        bgu = at(KV + 5888, F2)
        assert KV + 5888 + F2 <= HT
        y_out = hn
        lg = at(Q, TILES, E)
        top_v = at(Q + 96, TILES, 8)
        top_i = at(Q + 120, TILES, 8).bitcast(U32)
        top_f = at(Q + 144, TILES, 4)
        top_w = at(Q + 156, TILES, 4)
        hot = at(Q + 168, TILES, 4, E)
        hotw = at(Q + 552, TILES, 4, E)
        picked = at(Q + 936, TILES, E)
        pair_n = at(Q + 1032, PAIRS)
        flag = at(Q + 1048, 4, PAIRS)
        n_over_f = at(Q + 1112, 1)
        n_over_i = at(Q + 1113, 1).bitcast(I32)
        before = at(Q + 1114, 2, 64)
        work = at(Q + 1242, EXTRA, 64)
        work_f = at(Q + 2394, 2, EXTRA)
        work_i = at(Q + 2430, 2, EXTRA).bitcast(I32)
        pair_of = at(Q + 2466, 64)
        round_of = at(Q + 2530, 64)
        picked_off = at(Q + 2594, TILES, E)
        late = at(Q + 3328 - late_cols, late_cols)
        assert Q + 3328 - late_cols >= Q + 2690

        def late_const(name):
            a, n = table[name]
            return late[:, a - ncols:a - ncols + n]

        iota, earlier, ones = late_const("iota"), late_const("earlier"), late_const("ones")
        rw = at(MX, KC, E)
        rb = at(MX + 256, E)
        rankm = at(MX + 288, TILES, E + 2)
        gates = at(MX + 390, TILES, E + 2)

        x_p = t["x_prompt"][0].rearrange("(t p) d -> p t d", p=P)
        x_s = t["x_sample"].rearrange("s i d -> (s i) d")
        w_in = t["w_in"][0].rearrange("(k p) e -> p k e", p=P)
        w_out = t["w_out"][0].rearrange("(k p) e -> p k e", p=P)
        w_gu = t["w_gate_up"][0]
        w_dn = t["w_down"][0]
        ck = t["cache_k"][0].rearrange("n p h d -> n p (h d)")
        cv = t["cache_v"][0].rearrange("n p h d -> n p (h d)")
        n_phys = ck.shape[0]
        BLOCKS = [4, 5, 6, 0, 1, 2, 3]
        SLOT = [0, 1, 2, 0, 1, 2, 0]

        late_in, st2_stored = sem("late_in"), sem("st2_stored")
        consts_in, x_in, gains_in, pages_in, router_in = map(sem, (
            "consts_in", "x_in", "gains_in", "pages_in", "router_in"))
        win_in = [sem(f"win_in{i}") for i in range(3)]
        kv_in = [sem(f"kv_in{i}") for i in range(4)]
        state_in, y_in, fg_in, bias_in = map(sem, ("state_in", "y_in", "fg_in", "bias_in"))
        a_full, a_empty, d_full, d_empty = map(sem, ("a_full", "a_empty", "d_full", "d_empty"))
        act_step, dve_step, pool_step = map(sem, ("act_step", "dve_step", "pool_step"))
        zeroed = sem("zeroed")
        x_rstd, x_scaled, qblk_ready = map(sem, ("x_rstd", "x_scaled", "qblk_ready"))
        own_full, own_ready = sem("own_full"), sem("own_ready")
        qk_done, s_evac = sem("qk_done"), sem("s_evac")
        soft_bias, probs_ready, own_probs = map(sem, ("soft_bias", "probs_ready", "own_probs"))
        v_used, o_norm = sem("v_used"), sem("o_norm")
        p_bias, p_exp, p_probs = map(sem, ("p_bias", "p_exp", "p_probs"))
        mvs_ready, mk_stored, mv_stored = map(sem, ("mvs_ready", "mk_stored", "mv_stored"))
        rot_done, kdec_ready, qdec_ready, vblk_ready = map(sem, (
            "rot_done", "kdec_ready", "qdec_ready", "vblk_ready"))
        state_new, state_stored, st2_ready = map(sem, ("state_new", "state_stored", "st2_ready"))
        sig_ready, var_ready, std_ready, ret_ready = map(sem, (
            "sig_ready", "var_ready", "std_ready", "ret_ready"))
        wout_s, y_ready, y_std, y_rstd, hn_ready = map(sem, (
            "wout_s", "y_ready", "y_std", "y_rstd", "hn_ready"))
        lg_full, d4_ready, e4_ready, gates_ready, rank_full = map(sem, (
            "lg_full", "d4_ready", "e4_ready", "gates_ready", "rank_full"))
        gt_full, rank_ready, moe_zero = map(sem, ("gt_full", "rank_ready", "moe_zero"))
        over_ready, work_ready = sem("over_ready"), sem("work_ready")
        gu_in = [sem(f"gu_in{i}") for i in range(KC)]
        dn_in = [sem(f"dn_in{i}") for i in range(4)]
        gu_used, dn_used, u_read, esel_ready = map(sem, (
            "gu_used", "dn_used", "u_read", "esel_ready"))
        glu_ready, sigm_ready, a_ready, at_full, at_ready, out_ready = map(sem, (
            "glu_ready", "sigm_ready", "a_ready", "at_full", "at_ready", "out_ready"))
        comb_full, comb_added, sgt_full, sgt_ready = map(sem, (
            "comb_full", "comb_added", "sgt_full", "sgt_ready"))
        lin_ready, selg_eq, qdm_zero = sem("lin_ready"), sem("selg_eq"), sem("qdm_zero")
        sel_ready, selg_ready, x_full, xnat_ready, xt_full, xt_ready = map(sem, (
            "sel_ready", "selg_ready", "x_full", "xnat_ready", "xt_full", "xt_ready"))
        sq_ready, f_rstd, yo_ready, stored = map(sem, ("sq_ready", "f_rstd", "yo_ready", "stored"))
        mark = {}

        block = ctx.enter_context(nc.Block())

        def wait_all(engine, marks):
            for semaphore, value in marks:
                engine.wait_ge(semaphore, value)

        def extra_pairs(engine):
            engine.wait_ge(over_ready, 1)
            return engine.value_load(n_over_i[0:1, 0:1], min_val=0, max_val=EXTRA)

        @block.tensor
        def _(pe):
            A = Ring((0, 1), a_full, a_empty)
            V = Ring((2, 3), d_full, d_empty)
            mm, tr = nc.tensor.matmul, nc.tensor.transpose

            def transposes(ring, blocks, rows=P):
                ring.wait_empty(pe)
                b = ring.bank()
                col = 0
                for src in blocks:
                    m = src.shape[1]
                    last = tr(psum[0:m, b, col:col + rows], src, ident[0:rows, 0:rows])
                    col += rows
                return ring.filled(last)

            def project(b):
                w = win[:, b % 3]
                pe.wait_ge(win_in[b % 3], 16 * (b // 3 + 1))
                lhs = h_t
                marks = []
                for tile, ring in ((0, A), (1, V)):
                    ring.wait_empty(pe)
                    for k in range(KC):
                        last = mm(psum[:, ring.bank(), :], lhs[:, k, tile * P:(tile + 1) * P],
                                  w[:, k, :], start=k == 0, stop=k == KC - 1)
                    marks.append((ring, ring.filled(last)))
                ring = V if b % 2 else A
                ring.wait_empty(pe)
                for k in range(KC):
                    for j in range(4):
                        last = mm(psum[NS * j:NS * (j + 1), ring.bank(), 0:P],
                                  lhs[:, k, LP:TOK], w[:, k, j * P:(j + 1) * P],
                                  start=k == 0, stop=k == KC - 1)
                marks.append((ring, ring.filled(last)))
                mark[f"block{b}"] = (ring.full, ring.n)
                mark[f"z{b}"] = [(r.empty, n) for r, n in marks]
                return marks

            def evacuated(marks):
                for ring, n in marks:
                    pe.wait_ge(ring.empty, n)

            def z_transposes(slot, sample_ring, before=()):
                got = []
                for tile, ring in ((0, A), (1, V), (2, sample_ring)):
                    r = COLS[tile]
                    n = transposes(ring, [z[0:r, slot, tile, c * P:(c + 1) * P] for c in range(4)], r)
                    got.append((ring, n))
                return got

            pe.sem_inc(qk_done, 2)
            pe.sem_inc(s_evac, 1)
            pe.sem_inc(u_read, 1)
            pe.wait_ge(consts_in, 16)
            pe.wait_ge(gains_in, 48)
            transposes(V, [gain_in[0:20, :]], 20)
            for tile in range(2):
                pe.wait_ge(x_scaled, tile + 1)
                for ring, k0 in ((A, 0), (V, 4)):
                    n = transposes(ring, [x_sb[:, tile, k * P:(k + 1) * P] for k in range(k0, k0 + 4)])
            pe.wait_ge(x_scaled, 3)
            n_x = transposes(A, [x_sb[0:NS, 2, k * P:(k + 1) * P] for k in range(KC)], NS)
            pe.wait_ge(a_empty, n_x)
            pe.wait_ge(d_empty, V.n)
            mq = project(0)
            mk = project(1)
            evacuated(mq)
            mqt = z_transposes(0, A)
            evacuated(mk)
            mark["mq_t"] = [(r.empty, n) for r, n in mqt]
            mkt = z_transposes(1, V)
            mv = project(2)
            pe.wait_ge(qblk_ready, 1)
            evacuated(mkt)
            for g in range(2):
                for c in range(4):
                    for s in range(4):
                        last = mm(psum[NS * s:NS * (s + 1), 5, NS * g:NS * (g + 1)],
                                  q_blk[:, 4 * g + s, c, :], mk_t[:, c, LP:TOK],
                                  start=c == 0, stop=c == 3)
            last.then_inc(own_full, 1)

            mark["k_base"] = V.n
            for g in range(2):
                a0, v0 = A.n, V.n
                with pe.Fori(0, 4) as i:
                    A.loop(i * 8)
                    V.loop(i * 8)

                    def scores(j):
                        pe.wait_ge(a_empty, i * 8 + (a0 + 2 * j + 2))
                        pe.wait_ge(d_empty, i * 8 + (v0 + 2 * j + 2))
                        if j == 0:
                            pe.wait_ge(s_evac, i + (4 * g + 1))
                        for c in range(4):
                            for s in range(4):
                                last = mm(psum[NS * s:NS * (s + 1), 4, P * j:P * (j + 1)],
                                          q_blk[:, 4 * g + s, c, :], kt_sb[:, j % 2, s, c, :],
                                          start=c == 0, stop=c == 3)
                        last.then_inc(qk_done, 1)

                    for j in range(4):
                        pe.wait_ge(kv_in[j], i * 64 + 64 * (4 * g + 1))
                        for s in range(4):
                            transposes(A if s < 2 else V,
                                       [kv[:, j, s, c * P:(c + 1) * P] for c in range(4)])
                        if j:
                            scores(j - 1)
                    scores(3)
                A.leave(4, 8)
                V.leave(4, 8)

            def p_transposes(v):
                g, q = v // 4, v % 4
                pe.wait_ge(probs_ready, g + 1)
                n = transposes(A, [s_raw[:, g, (4 * q + j) * P:(4 * q + j + 1) * P] for j in range(4)])
                mark[f"pt{v}"] = (a_full, n)
                return n

            def own_transposes(g):
                pe.wait_ge(own_probs, g + 1)
                V.wait_empty(pe)
                return V.filled(tr(psum[0:NS, V.bank(), 0:P], own_s[:, g, :], ident))

            def values(v, n_pt, n_own=None):
                g, q = v // 4, v % 4
                pe.wait_ge(a_empty, n_pt)
                if q == 0:
                    pe.wait_ge(d_empty, n_own)
                    pe.wait_ge(mvs_ready, 1)
                    for s in range(4):
                        mm(psum[NS * s:NS * (s + 1), 6 + g, :], pt_own[0:NS, g, NS * s:NS * (s + 1)],
                           mv_s[0:NS, :], start=True, stop=False, skip_group_check=True)
                for j in range(4):
                    pe.wait_ge(kv_in[j], 64 * (8 + v + 1))
                    for s in range(4):
                        last = mm(psum[NS * s:NS * (s + 1), 6 + g, :],
                                  pt_sb[:, v % 2, j * P + NS * s:j * P + NS * (s + 1)],
                                  kv[:, j, s, :], start=False, stop=q == 3 and j == 3,
                                  skip_group_check=True)
                    last.then_inc(v_used, 1)

            def o_transposes(g):
                pe.wait_ge(o_norm, g + 1)
                n = transposes(V, [o_sb[g][:, c * P:(c + 1) * P] for c in range(4)])
                mark[f"o_t{g}"] = (d_full, n)

            project(3)
            pt = p_transposes(0)
            po = own_transposes(0)
            for u in range(6):
                V.wait_empty(pe)
                heads = HEADS0[4 * u:4 * u + 4] if u < 2 else HEADS1[2 * (u - 2):2 * (u - 2) + 2]
                for n, h in enumerate(heads):
                    r = 64 * (h % 2)
                    tile, w = (0, P) if u < 2 else (1, LP)
                    last = mm(psum[:, V.bank(), n * w:(n + 1) * w],
                              mq_t[r:r + 64, h // 2, tile * P:(tile + 1) * P],
                              mk_t[r:r + 64, h // 2, 0:w], start=True, stop=True)
                V.filled(last)
            values(0, pt, po)
            pt = p_transposes(1)
            project(4)
            values(1, pt)
            pt = p_transposes(2)
            pe.wait_ge(p_probs, 1)
            for u in range(6):
                n = transposes(V if u % 2 else A, [s_prompt[:, 4 * u + j, :] for j in range(4)])
            values(2, pt)
            pe.wait_ge(a_empty, A.n)
            pe.wait_ge(d_empty, V.n)
            evacuated(mv)
            for half, ring in ((0, A), (1, V)):
                ring.wait_empty(pe)
                b = ring.bank()
                for c in range(2):
                    for u in range(2):
                        h = 2 * (2 * half + c) + u
                        o = psum[64 * u:64 * (u + 1), b, c * LP:(c + 1) * LP]
                        n0, n1 = HEADS0.index(h), 8 + 2 * HEADS1.index(h)
                        mm(o[:, 0:P], z[:, 2, 0, 64 * h:64 * (h + 1)], pt_prompt[:, n0, :],
                           start=True, stop=True)
                        mm(o[:, P:LP], z[:, 2, 0, 64 * h:64 * (h + 1)], pt_prompt[:, n1, :],
                           start=True, stop=False)
                        last = mm(o[:, P:LP], z[:, 2, 1, 64 * h:64 * (h + 1)],
                                  pt_prompt[:, n1 + 1, :], start=False, stop=True)
                ring.filled(last)
            mark["prompt_o"] = [(A.full, A.n), (V.full, V.n)]
            pt = p_transposes(3)
            rv = project(5)
            values(3, pt)
            pt = p_transposes(4)
            po = own_transposes(1)
            project(6)
            values(4, pt, po)
            o_transposes(0)
            pe.wait_ge(rot_done, 2)
            rt = []
            for src, sample_ring in ((rot_q, A), (rot_k, V)):
                for tile, ring in ((0, A), (1, V), (2, sample_ring)):
                    r = COLS[tile]
                    rt.append((ring, transposes(ring, [src[0:r, tile, c, :] for c in range(4)], r)))
            pe.wait_ge(qdec_ready, 1)
            rt.append((A, transposes(A, [q_dec[:, 0, c, :] for c in range(4)])))
            rt.append((V, transposes(V, [q_dec[0:NS, 1, c, :] for c in range(4)], NS)))
            mark["ret_t"] = [(A.full, A.n), (V.full, V.n)]
            pt = p_transposes(5)
            values(5, pt)
            evacuated(rt)
            sc = []
            for tile in range(3):
                w = COLS[tile]
                lo = tile * P
                V.wait_empty(pe)
                for h in range(RH):
                    last = mm(psum[0:w, V.bank(), h * w:(h + 1) * w], rk_t[:, h, lo:lo + w],
                              rq_t[:, h, lo:lo + w], start=True, stop=True)
                sc.append(V.filled(last))
            pe.wait_ge(kdec_ready, 1)
            evacuated(rv)
            for tile, ring in ((0, A), (1, V)):
                ring.wait_empty(pe)
                for h in range(RH):
                    last = mm(psum[:, ring.bank(), h * P:(h + 1) * P], k_dec[:, tile, h, :],
                              z[:, 2, tile, h * P:(h + 1) * P], start=True, stop=True)
                n = ring.filled(last)
                if tile == 0:
                    n_st1 = n
                    mark["st1"] = (a_empty, n)
            pt = p_transposes(6)
            values(6, pt)
            pe.wait_ge(d_empty, sc[2])
            pe.wait_ge(a_empty, n_st1)
            pe.wait_ge(state_in, 16)
            for tile in range(3):
                w = COLS[tile]
                A.wait_empty(pe)
                for h in range(RH):
                    o = psum[0:w, A.bank(), h * P:(h + 1) * P]
                    inner = sc_p[:, tile, h, :] if tile < 2 else sc_s[0:NS, h, :]
                    last = mm(o, inner, z[0:w, 2, tile, h * P:(h + 1) * P],
                              start=True, stop=tile == 0, skip_group_check=True)
                    if tile == 1:
                        last = mm(o, qd_t[:, h, :], st1[:, h, :], start=False, stop=True,
                                  skip_group_check=True)
                    if tile == 2:
                        for s in range(SEQS):
                            last = mm(o, qdm_flat[:, h, NS * s:NS * (s + 1)], state[:, s, h, :],
                                      start=False, stop=s == SEQS - 1, skip_group_check=True)
                mark["ret_out"] = (a_empty, A.filled(last))
            for h in range(RH):
                pe.wait_ge(vblk_ready, h + 1)
                for half in range(2):
                    V.wait_empty(pe)
                    last = mm(psum[:, V.bank(), :], k_dec[0:NS, 2, h, :],
                              v_blk[0:NS, 4 * half:4 * half + 4, :], start=True, stop=True)
                    V.filled(last)
                mark[f"vblk{h}"] = (V.full, V.n)
            pt = p_transposes(7)
            values(7, pt)
            pe.wait_ge(ret_ready, 1)
            for tile, ring in ((0, A), (1, V), (2, A)):
                r = COLS[tile]
                transposes(ring, [tmp[0:r, tile, c, :] for c in range(4)], r)
            o_transposes(1)
            pe.wait_ge(a_empty, A.n)
            pe.wait_ge(d_empty, V.n)
            for half in range(2):
                b = 7 + half
                pe.wait_ge(win_in[b % 3], 16 * (b // 3 + 1))
                for tile, ring in ((0, V), (1, V), (2, A)):
                    w = COLS[tile]
                    ring.wait_empty(pe)
                    for k in range(KC):
                        if tile < 2:
                            last = mm(psum[:, ring.bank(), :], mix_t[:, k, tile * P:(tile + 1) * P],
                                      win[:, b % 3, k, :], start=k == 0, stop=k == KC - 1)
                        else:
                            for j in range(4):
                                last = mm(psum[NS * j:NS * (j + 1), ring.bank(), 0:P],
                                          mix_t[:, k, LP:TOK], win[:, b % 3, k, j * P:(j + 1) * P],
                                          start=k == 0, stop=k == KC - 1)
                    ring.filled(last)
                mark[f"w_out_s{half}"] = (a_empty, A.n)
            mark["w_out"] = (A.full, A.n)
            for tile in range(2):
                pe.wait_ge(hn_ready, tile + 1)
                for ring, k0 in ((A, 0), (V, 4)):
                    transposes(ring, [hn[:, tile, k * P:(k + 1) * P] for k in range(k0, k0 + 4)])
            pe.wait_ge(hn_ready, 3)
            transposes(A, [hn[0:NS, 2, k * P:(k + 1) * P] for k in range(KC)], NS)
            pe.wait_ge(a_empty, A.n)
            pe.wait_ge(d_empty, V.n)
            pe.wait_ge(router_in, 32)
            for tile in range(3):
                w = COLS[tile]
                for k in range(KC):
                    last = mm(psum[0:w, 4, E * tile:E * (tile + 1)], h2_t[:, k, tile * P:tile * P + w],
                              rw[:, k, :], start=k == 0, stop=k == KC - 1)
            last.then_inc(lg_full, 1)
            pe.wait_ge(late_in, 16)
            pe.wait_ge(gates_ready, 1)
            for tile in range(4):
                parts = [(ones, n) for n in range(min(tile, 3))]
                parts += [(earlier, tile)] if tile < 3 else []
                for n, (lhs, src) in enumerate(parts):
                    last = mm(psum[:, 5, E * tile:E * (tile + 1)], lhs, picked[:, src, :],
                              start=n == 0, stop=n == len(parts) - 1)
            last.then_inc(rank_full, 1)
            for tile in range(3):
                last = tr(psum[0:E, 6, P * tile:P * (tile + 1)], gates[:, tile, 0:E], ident)
            last.then_inc(gt_full, 1)

            def gather(n):
                pe.wait_ge(sel_ready, n + 1)
                for half in range(2):
                    for tile in range(3):
                        last = mm(psum[:, 3 + half, :], sel[:, tile].rearrange("p a b -> p (a b)"),
                                  hn[:, tile, 512 * half:512 * (half + 1)],
                                  start=tile == 0, stop=tile == 2)
                last.then_inc(x_full, 1)

            def gathered_transposes(n):
                pe.wait_ge(xnat_ready, n + 1)
                for k in range(KC):
                    last = tr(psum[:, 6 + k // 4, P * (k % 4):P * (k % 4 + 1)],
                              x_nat[:, k * P:(k + 1) * P], ident)
                last.then_inc(xt_full, 1)

            def combine(m):
                pe.wait_ge(sgt_ready, m + 1)
                pe.wait_ge(out_ready, m * 2 + 1)
                for u in range(6):
                    tile, half = u // 2, u % 2
                    if u >= 2:
                        pe.wait_ge(comb_added, m * 6 + (u - 1))
                    w = COLS[tile]
                    mm(psum[0:w, 3 + half, :], sgt[:, P * tile:P * tile + w],
                       out2[:, 512 * half:512 * (half + 1)], start=True, stop=True)\
                        .then_inc(comb_full, 1)

            def pair(n, ahead):
                pe.wait_ge(xt_ready, n + (1 if ahead else 2))
                pe.wait_ge(esel_ready, n + (1 if ahead else 2))
                for e in range(2):
                    pe.wait_ge(u_read, n * 2 + (e + 1))
                    lhs = slice(SLOTS * e, SLOTS * (e + 1))
                    for b in range(2):
                        for g in range(2):
                            c = 1024 * g + 512 * b
                            mm(psum[64 * g:64 * (g + 1), b, :], esel[:, e, :], bgu[:, c:c + 512],
                               start=True, stop=False, skip_group_check=True)
                    for k in range(KC):
                        pe.wait_ge(gu_in[k], n * 32 + 16 * (e + 1))
                        for b in range(2):
                            for g in range(2):
                                c = 1024 * g + 512 * b
                                last = mm(psum[64 * g:64 * (g + 1), b, :], xt[:, k, lhs],
                                          gu[:, k, c:c + 512], start=False, stop=k == KC - 1,
                                          skip_group_check=True)
                        last.then_inc(gu_used, 1)
                    if e == 0:
                        combine(n)
                        pe.wait_ge(selg_ready, n + 1)
                        for tile in range(3):
                            last = tr(psum[:, 7, P * tile:P * (tile + 1)],
                                      selg[:, tile].rearrange("p a b -> p (a b)"), ident)
                        last.then_inc(sgt_full, 1)
                    elif ahead:
                        pe.wait_ge(comb_added, n * 6 + 6)
                        gather(n + 1)
                    pe.wait_ge(a_ready, n * 2 + (e + 1))
                    for q in range(4):
                        last = tr(psum[:, 5, P * q:P * (q + 1)], a_sb[:, P * q:P * (q + 1)], ident)
                    last.then_inc(at_full, 1)
                    if e == 1 and ahead:
                        pe.wait_ge(sgt_ready, n + 2)
                        gathered_transposes(n + 1)
                    pe.wait_ge(at_ready, n * 2 + (e + 1))
                    pe.wait_ge(out_ready, n * 2 + (e + 1))
                    for m in range(KC):
                        if m % 2 == 0:
                            pe.wait_ge(dn_in[m // 2], n * 32 + 16 * (e + 1))
                        half, q = m // 4, m % 4
                        for g in range(2):
                            last = mm(psum[64 * g:64 * (g + 1), 2, :],
                                      at_sb[:, q, SLOTS * half:SLOTS * (half + 1)],
                                      dn[:, m, 512 * g:512 * (g + 1)],
                                      start=m == 0, stop=m == KC - 1)
                        if m % 2:
                            last.then_inc(dn_used, 1)

            pe.wait_ge(bias_in, 32)
            pe.sem_inc(out_ready, 1)
            pe.wait_ge(sgt_ready, 1)
            pe.sem_inc(sgt_full, 1)
            gather(0)
            gathered_transposes(0)
            with pe.Fori(0, PAIRS) as n:
                pair(n, True)
            more = extra_pairs(pe)
            with pe.If(more > 0):
                with pe.Fori(PAIRS, more + PAIRS) as n:
                    pe.wait_ge(comb_added, n * 6)
                    gather(n + 1)
                    gathered_transposes(n + 1)
                    pair(n, False)
            with pe.Else():
                pe.nop()
            pe.wait_ge(comb_added, more * 6 + 6 * PAIRS)
            combine(more + PAIRS)

        @block.scalar
        def _(act):
            A = Ring((0, 1), a_full, a_empty)
            chain = [0]

            def link(ins):
                chain[0] += 1
                ins.then_inc(act_step, 1)
                act.wait_ge(act_step, chain[0])

            def copy(out, in_, scale=1.0):
                return nc.scalar.activation(out, in_, ACT.Copy, scale=scale)

            def evacuate(out, rows=P, width=512):
                A.wait_full(act)
                A.emptied(copy(out, psum[0:rows, A.bank(), 0:width]))

            def evacuate_sample(out):
                A.wait_full(act)
                for j in range(4):
                    ins = copy(out[:, P * j:P * (j + 1)], psum[NS * j:NS * (j + 1), A.bank(), 0:P])
                A.emptied(ins)

            def evacuate_scaled(dst, w, tile, chunks, gains):
                A.wait_full(act)
                for n, k in enumerate(chunks):
                    ins = copy(dst[:, k, tile * P:tile * P + w],
                               psum[:, A.bank(), n * w:(n + 1) * w], scale=gains[:, k:k + 1])
                A.emptied(ins)

            def evacuate_t(dst, tile):
                w = COLS[tile]
                A.wait_full(act)
                A.emptied(copy(dst[:, 0:4, tile * P:tile * P + w],
                               psum[:, A.bank(), 0:4 * w].rearrange("p (c w) -> p c w", c=4)))

            act.wait_ge(zeroed, 1)
            act.wait_ge(consts_in, 16)
            act.wait_ge(x_in, 32)
            for tile in range(3):
                r = COLS[tile]
                ins = nc.scalar.activation(at(HT + 1024 * (tile % 2), D)[0:r], x_sb[0:r, tile, :], ACT.Square,
                                           accum_out=stat[0:r, tile:tile + 1])
                link(ins)
            nc.scalar.activation(stat[:, 3:6], stat[:, 0:3], ACT.Sqrt, scale=1.0 / D,
                                 bias=const("eps")).then_inc(x_rstd, 1)
            act.wait_ge(x_rstd, 2)
            for tile in range(3):
                r = COLS[tile]
                copy(x_sb[0:r, tile, :], x_sb[0:r, tile, :], scale=stat[0:r, 6 + tile:7 + tile])\
                    .then_inc(x_scaled, 1)
            act.wait_ge(d_empty, 1)
            evacuate_scaled(h_t, P, 0, range(4), gain)
            evacuate_scaled(h_t, P, 1, range(4), gain)
            evacuate_scaled(h_t, NS, 2, range(KC), gain)
            evacuate(z[:, 0, 0, :])
            evacuate_sample(z[0:NS, 0, 2, :])
            evacuate(z[:, 1, 0, :])
            evacuate_t(mq_t, 0)
            evacuate_t(mq_t, 2)
            evacuate_t(mk_t, 0)
            evacuate(z[:, 2, 0, :])
            evacuate_sample(z[0:NS, 2, 2, :])

            for g in range(2):
                with act.Fori(0, 4) as i:
                    A.loop(i * 8)
                    for j in range(4):
                        for s in range(2):
                            if s == 0:
                                act.wait_ge(qk_done, i * 4 + (16 * g + j + 1))
                            evacuate(kt_sb[:, j % 2, s].rearrange("p c t -> p (c t)"))
                    act.wait_ge(qk_done, i * 4 + (16 * g + 4 + 2))
                    copy(s_raw[:, g, bass.ds(i * 512, 512)], psum[:, 4, :]).then_inc(s_evac, 1)
                A.leave(4, 8)

            def probabilities(g):
                act.wait_ge(soft_bias, g + 1)
                for b in range(8):
                    s = s_raw[:, g, 256 * b:256 * (b + 1)]
                    ins = nc.scalar.activation(s, s, ACT.Exp, bias=sm[:, g, 24 + b:25 + b],
                                               scale=SCALE, accum_out=sm[:, g, 40 + b:41 + b])
                ins.then_inc(probs_ready, 1)
                nc.scalar.activation(own_s[:, g, :], own_s[:, g, :], ACT.Exp,
                                     bias=sm[:, g, 32:33], scale=SCALE,
                                     accum_out=sm[:, g, 48:49]).then_inc(own_probs, 1)

            def evacuate_pt(v):
                if v >= 2:
                    act.wait_ge(v_used, 4 * (v - 1))
                evacuate(pt_sb[:, v % 2, :])

            probabilities(0)
            evacuate(z[:, 0, 0, :])
            evacuate_pt(0)
            act.wait_ge(p_bias, 1)
            for b in range(MH):
                ins = nc.scalar.activation(s_prompt[:, b, :], s_prompt[:, b, :], ACT.Exp,
                                           bias=pm[:, 16 + b:17 + b], scale=SCALE,
                                           accum_out=pm[:, 32 + b:33 + b])
            for h in range(MH):
                s = s_prompt[:, 8 + 2 * h:10 + 2 * h, :]
                ins = nc.scalar.activation(s, s, ACT.Exp, bias=pm[:, 24 + h:25 + h], scale=SCALE,
                                           accum_out=pm[:, 40 + h:41 + h])
            ins.then_inc(p_exp, 1)
            evacuate_pt(1)
            act.wait_ge(mk_stored, 32)
            evacuate(z[:, 1, 0, :])
            evacuate_sample(z[0:NS, 1, 2, :])
            evacuate_pt(2)
            for u in range(0, 6, 2):
                evacuate(pt_prompt[:, 4 * u:4 * u + 4, :].rearrange("p b t -> p (b t)"))
            probabilities(1)
            A.wait_full(act)
            A.emptied(copy(mix_t[:, 4:6, 0:LP], psum[:, A.bank(), :].rearrange("p (c w) -> p c w", c=2)))
            evacuate_pt(3)
            act.wait_ge(mv_stored, 32)
            act.wait_ge(mvs_ready, 1)
            evacuate(z[:, 2, 0, :])
            evacuate_pt(4)
            act.wait_ge(rot_done, 1)
            evacuate(z[:, 0, 0, :])
            evacuate_sample(z[0:NS, 0, 2, :])
            evacuate_t(rq_t, 0)
            evacuate_t(rq_t, 2)
            evacuate_t(rk_t, 0)
            evacuate(qd_t.rearrange("p h t -> p (h t)"))
            evacuate_pt(5)
            evacuate(st1.rearrange("p h t -> p (h t)"))
            evacuate_pt(6)
            act.wait_ge(qdec_ready, 1)
            act.wait_ge(kdec_ready, 1)
            for tile in range(3):
                evacuate(ret_o[0:COLS[tile], tile].rearrange("p h d -> p (h d)"), rows=COLS[tile])
            wait_all(act, mark["z6"])
            nc.scalar.activation(sig_g, z[:, 0].rearrange("p t (h d) -> p t h d", h=RH),
                                 ACT.Sigmoid).then_inc(sig_ready, 1)
            evacuate_pt(7)
            act.wait_ge(var_ready, 1)
            nc.scalar.activation(stat[:, 36:48], stat[:, 24:36], ACT.Sqrt, scale=1.0 / P,
                                 bias=const("eps")).then_inc(std_ready, 1)
            evacuate_scaled(mix_t, P, 0, range(4), gain[:, 16:20])
            evacuate_scaled(mix_t, NS, 2, range(4), gain[:, 16:20])
            for half in range(2):
                if half:
                    act.wait_ge(wout_s, 1)
                evacuate_sample(mv_s[0:NS, :])
            act.wait_ge(y_ready, 1)
            for tile in range(3):
                link(nc.scalar.activation(x_nat, y[:, tile, :], ACT.Square,
                                          accum_out=stat[:, 9 + tile:10 + tile]))
            nc.scalar.activation(stat[:, 12:15], stat[:, 9:12], ACT.Sqrt, scale=1.0 / D,
                                 bias=const("eps")).then_inc(y_std, 1)
            act.wait_ge(y_rstd, 1)
            for tile in range(3):
                copy(hn[:, tile, :], y[:, tile, :], scale=stat[:, 15 + tile:16 + tile])\
                    .then_inc(hn_ready, 1)
            act.wait_ge(st2_stored, 16)
            evacuate_scaled(h2_t, P, 0, range(4), gain[:, 8:16])
            evacuate_scaled(h2_t, P, 1, range(4), gain[:, 8:16])
            evacuate_scaled(h2_t, NS, 2, range(KC), gain[:, 8:16])
            act.wait_ge(d4_ready, 1)
            nc.scalar.activation(top_w, top_w, ACT.Exp).then_inc(e4_ready, 1)

            def gathered(n):
                act.wait_ge(x_full, n + 1)
                copy(x_nat.rearrange("p (a b) -> p a b", a=2), psum[:, 3:5, :]).then_inc(xnat_ready, 1)

            def gathered_t(n):
                act.wait_ge(xt_full, n + 1)
                for k in range(KC):
                    ins = copy(xt[:, k, :], psum[:, 6 + k // 4, P * (k % 4):P * (k % 4 + 1)],
                               scale=gain[:, 8 + k:9 + k])
                ins.then_inc(xt_ready, 1)

            def pair(n, ahead):
                for e in range(2):
                    act.wait_ge(glu_ready, n * 2 + (e + 1))
                    nc.scalar.activation(sg_sb, g_sb, ACT.Sigmoid, scale=ALPHA).then_inc(sigm_ready, 1)
                    if e == 0:
                        act.wait_ge(sgt_full, n + 2)
                        copy(sgt, psum[:, 7, 0:TILES * P]).then_inc(sgt_ready, 1)
                    elif ahead:
                        gathered(n + 1)
                    act.wait_ge(at_full, n * 2 + (e + 1))
                    copy(at_sb.rearrange("p q t -> p (q t)"), psum[:, 5, :]).then_inc(at_ready, 1)
                    if e == 1 and ahead:
                        gathered_t(n + 1)
                    act.wait_ge(dn_used, n * 8 + 4 * (e + 1))
                    for g in range(2):
                        ins = copy(out2[64 * e:64 * (e + 1), 512 * g:512 * (g + 1)],
                                   psum[64 * g:64 * (g + 1), 2, :])
                    ins.then_inc(out_ready, 1)

            gathered(0)
            gathered_t(0)
            with act.Fori(0, PAIRS) as n:
                pair(n, True)
            more = extra_pairs(act)
            with act.If(more > 0):
                with act.Fori(PAIRS, more + PAIRS) as n:
                    gathered(n + 1)
                    gathered_t(n + 1)
                    pair(n, False)
            with act.Else():
                act.nop()
            act.wait_ge(comb_added, more * 6 + 6 * (PAIRS + 1))
            for tile in range(3):
                link(nc.scalar.activation(x_nat, y[:, tile, :], ACT.Square,
                                          accum_out=stat[:, 50 + tile:51 + tile]))
            nc.scalar.activation(stat[:, 53:56], stat[:, 50:53], ACT.Sqrt, scale=1.0 / D,
                                 bias=const("eps")).then_inc(sq_ready, 1)

        @block.vector
        def _(dve):
            V = Ring((2, 3), d_full, d_empty)
            v = nc.vector
            chain = [0]

            def link(ins):
                chain[0] += 1
                ins.then_inc(dve_step, 1)
                dve.wait_ge(dve_step, chain[0])

            def evacuate(out, rows=P, width=512):
                V.wait_full(dve)
                V.emptied(v.tensor_copy(out, psum[0:rows, V.bank(), 0:width]))

            def evacuate_sample(out):
                V.wait_full(dve)
                for j in range(4):
                    ins = v.tensor_copy(out[:, P * j:P * (j + 1)], psum[NS * j:NS * (j + 1), V.bank(), 0:P])
                V.emptied(ins)

            def evacuate_scaled(dst, w, tile, chunks, gains):
                V.wait_full(dve)
                for n, k in enumerate(chunks):
                    ins = v.tensor_scalar(dst[:, k, tile * P:tile * P + w],
                                          psum[:, V.bank(), n * w:(n + 1) * w],
                                          gains[:, k:k + 1], None, ALU.mult)
                V.emptied(ins)

            def evacuate_t(dst, tile):
                w = COLS[tile]
                V.wait_full(dve)
                V.emptied(v.tensor_copy(dst[:, 0:4, tile * P:tile * P + w],
                                        psum[:, V.bank(), 0:4 * w].rearrange("p (c w) -> p c w", c=4)))

            evacuate(gain, width=20)
            dve.wait_ge(x_rstd, 1)
            v.reciprocal(stat[:, 6:9], stat[:, 3:6]).then_inc(x_rstd, 1)
            dve.wait_ge(d_empty, 1)
            evacuate_scaled(h_t, P, 0, range(4, 8), gain)
            evacuate_scaled(h_t, P, 1, range(4, 8), gain)
            evacuate(z[:, 0, 1, :])
            evacuate(z[:, 1, 1, :])
            evacuate_sample(z[0:NS, 1, 2, :])
            evacuate_t(mq_t, 1)
            evacuate_t(mk_t, 1)
            evacuate_t(mk_t, 2)
            evacuate(z[:, 2, 1, :])
            dve.wait_ge(own_full, 1)
            v.tensor_tensor(own_s.rearrange("p g t -> p (g t)"), psum[:, 5, 0:2 * NS],
                            const("own_mask"), ALU.add).then_inc(own_ready, 1)

            for g in range(2):
                with dve.Fori(0, 4) as i:
                    V.loop(i * 8)
                    for j in range(4):
                        for s in range(2, 4):
                            if s == 2:
                                dve.wait_ge(qk_done, i * 4 + (16 * g + j + 1))
                            evacuate(kt_sb[:, j % 2, s].rearrange("p c t -> p (c t)"))
                V.leave(4, 8)

            def choose(g):
                dve.wait_ge(s_evac, 4 * (g + 1) + 1)
                s = s_raw[:, g, :].rearrange("p (b t) -> p b t", b=8)
                w = sm[:, g, :]
                gate, peak, bias = w[:, 0:8], w[:, 8:16], w[:, 24:32]
                v.reduce_sum(gate, s, axis=AXX)
                link(v.reduce_max(peak, s, axis=AXX))
                other = gate.unsqueeze(1).broadcast_to([P, 8, 8])
                this = gate.unsqueeze(2).broadcast_to([P, 8, 8])
                gt, eq = cmp[:, 0], cmp[:, 1]
                v.tensor_tensor(gt, other, this, ALU.is_gt)
                link(v.tensor_tensor(eq, other, this, ALU.is_equal))
                link(v.tensor_tensor(eq, eq, const("before8").rearrange("p (j i) -> p j i", j=8), ALU.mult))
                link(v.tensor_tensor(gt, gt, eq, ALU.add))
                link(v.reduce_sum(w[:, 16:24], gt, axis=AXX))
                link(v.tensor_scalar(bias, w[:, 16:24], 2.5, NEG, ALU.is_gt, ALU.mult))
                link(v.tensor_tensor(peak, peak, bias, ALU.add))
                v.reduce_max(w[:, 34:35], peak, axis=AXX)
                link(v.reduce_max(w[:, 35:36], own_s[:, g, :], axis=AXX))
                link(v.reduce_max(w[:, 33:34], w[:, 34:36], axis=AXX))
                link(v.tensor_scalar(w[:, 32:33], w[:, 33:34], -SCALE, None, ALU.mult))
                v.tensor_scalar(bias, bias, w[:, 32:33], None, ALU.add).then_inc(soft_bias, 1)

            def normalise(g):
                dve.wait_ge(own_probs, g + 1)
                w = sm[:, g, :]
                link(v.reduce_sum(w[:, 49:50], w[:, 40:49], axis=AXX))
                link(v.reciprocal(w[:, 50:51], w[:, 49:50]))
                dve.wait_ge(v_used, 16 * (g + 1))
                v.tensor_scalar(o_sb[g], psum[:, 6 + g, :], w[:, 50:51], None, ALU.mult).then_inc(o_norm, 1)

            def heads_to_mix(g):
                V.wait_full(dve)
                ps = psum[:, V.bank(), :].rearrange("p (c s h i) -> p c s h i", c=4, s=4, h=MH)
                for c in range(4):
                    for u in range(2):
                        dst = mix_t[64 * u:64 * (u + 1), 4 + c, LP + 16 * g:LP + 16 * (g + 1)]
                        ins = v.tensor_copy(dst.rearrange("p (s i) -> p s i", s=4),
                                            ps[64 * u:64 * (u + 1), c, :, 2 * c + u, :])
                V.emptied(ins)

            def evacuate_own(g):
                evacuate(pt_own[0:NS, g, :], rows=NS, width=P)

            choose(0)
            evacuate(z[:, 0, 1, :])
            evacuate_sample(z[0:NS, 0, 2, :])
            evacuate_own(0)
            causal = const("causal")
            for u in range(6):
                V.wait_full(dve)
                if u < 2:
                    ins = v.tensor_tensor(s_prompt[:, 4 * u:4 * u + 4, :],
                                          psum[:, V.bank(), :].rearrange("p (b t) -> p b t", b=4),
                                          causal.unsqueeze(1).broadcast_to([P, 4, P]), ALU.add)
                else:
                    h = 2 * (u - 2)
                    dst = s_prompt[:, 8 + 2 * h:12 + 2 * h, :].rearrange("p (h b) t -> p h b t", h=2)
                    src = psum[:, V.bank(), :].rearrange("p (h b t) -> p h b t", h=2, b=2)
                    v.tensor_copy(dst[:, :, 0, :], src[:, :, 0, :])
                    ins = v.tensor_tensor(dst[:, :, 1, :], src[:, :, 1, :],
                                          causal.unsqueeze(1).broadcast_to([P, 2, P]), ALU.add)
                n = V.emptied(ins)
            dve.wait_ge(d_empty, n)
            v.reduce_max(pm[:, 0:8], s_prompt[:, 0:8, :], axis=AXX)
            link(v.reduce_max(pm[:, 8:16], s_prompt[:, 8:24, :].rearrange("p (h b) t -> p h (b t)", h=8), axis=AXX))
            v.tensor_scalar(pm[:, 16:32], pm[:, 0:16], -SCALE, None, ALU.mult).then_inc(p_bias, 1)
            dve.wait_ge(mk_stored, 32)
            evacuate(z[:, 1, 1, :])
            dve.wait_ge(p_exp, 1)
            link(v.reciprocal(pm[:, 48:64], pm[:, 32:48]))
            v.tensor_tensor(s_prompt[:, 0:8, :], s_prompt[:, 0:8, :],
                            pm[:, 48:56].unsqueeze(2).broadcast_to([P, 8, P]), ALU.mult)
            s1 = s_prompt[:, 8:24, :].rearrange("p (h b) t -> p h (b t)", h=8)
            v.tensor_tensor(s1, s1, pm[:, 56:64].unsqueeze(2).broadcast_to([P, 8, LP]), ALU.mult)\
                .then_inc(p_probs, 1)
            for u in range(1, 6, 2):
                evacuate(pt_prompt[:, 4 * u:4 * u + 4, :].rearrange("p b t -> p (b t)"))
            choose(1)
            V.wait_full(dve)
            V.emptied(v.tensor_copy(mix_t[:, 6:8, 0:LP],
                                    psum[:, V.bank(), :].rearrange("p (c w) -> p c w", c=2)))
            dve.wait_ge(mv_stored, 32)
            dve.wait_ge(mvs_ready, 1)
            evacuate(z[:, 2, 1, :])
            evacuate_sample(z[0:NS, 2, 2, :])
            evacuate_own(1)
            dve.wait_ge(rot_done, 1)
            evacuate(z[:, 0, 1, :])
            normalise(0)
            heads_to_mix(0)
            evacuate_t(rq_t, 1)
            evacuate_t(rk_t, 1)
            evacuate_t(rk_t, 2)
            dve.wait_ge(qdm_zero, 1)
            V.wait_full(dve)
            V.emptied(v.tensor_copy(
                qdm[:, :, :, 0:4],
                psum[:, V.bank(), 0:P].rearrange("p (h s i) -> p h s i", h=RH, s=SEQS)))
            for tile in range(2):
                V.wait_full(dve)
                V.emptied(v.tensor_tensor(sc_p[:, tile].rearrange("p h t -> p (h t)"), psum[:, V.bank(), :],
                                          const("decay"), ALU.mult))
            V.wait_full(dve)
            V.emptied(v.tensor_tensor(sc_s[0:NS].rearrange("p h t -> p (h t)"), psum[0:NS, V.bank(), 0:P],
                                      const("decay_s")[0:NS], ALU.mult))
            V.wait_full(dve)
            dve.wait_ge(*mark["st1"])
            for h in range(RH):
                ins = v.scalar_tensor_tensor(st2[:, h, :], st1[:, h, :], GAMMA[h] ** P,
                                             psum[:, V.bank(), h * P:(h + 1) * P], ALU.mult, ALU.add)
            dve.wait_ge(d_empty, V.emptied(ins))
            dve.sem_inc(st2_ready, 1)
            for h in range(RH):
                for half in range(2):
                    V.wait_full(dve)
                    s = state[:, 4 * half:4 * half + 4, h, :]
                    V.emptied(v.scalar_tensor_tensor(
                        s, s, GAMMA[h] ** 4, psum[:, V.bank(), :].rearrange("p (s d) -> p s d", s=4),
                        ALU.mult, ALU.add))
            dve.wait_ge(d_empty, V.n)
            dve.sem_inc(state_new, 1)
            ro, tm = (w.rearrange("p t h d -> p (t h) d") for w in (ret_o, tmp))
            dve.wait_ge(*mark["ret_out"])
            red = pm[:, 0:12]
            link(v.reduce_sum(red, ro, axis=AXX))
            link(v.tensor_scalar(red, red, 1.0 / P, None, ALU.mult))
            link(v.tensor_tensor(ro, ro, red.unsqueeze(2).broadcast_to([P, 12, P]), ALU.subtract))
            link(v.tensor_tensor(tm, ro, ro, ALU.mult))
            link(v.reduce_sum(stat[:, 24:36], tm, axis=AXX))
            dve.sem_inc(var_ready, 1)
            dve.wait_ge(sig_ready, 1)
            zg = z[:, 0].rearrange("p t (h d) -> p (t h) d", h=RH)
            sg = sig_g.rearrange("p t h d -> p (t h) d")
            link(v.tensor_tensor(sg, sg, zg, ALU.mult))
            link(v.tensor_tensor(ro, ro, sg, ALU.mult))
            dve.wait_ge(std_ready, 1)
            link(v.reciprocal(red, stat[:, 36:48]))
            v.tensor_tensor(tm, ro, red.unsqueeze(2).broadcast_to([P, 12, P]), ALU.mult)\
                .then_inc(ret_ready, 1)
            evacuate_scaled(mix_t, P, 1, range(4), gain[:, 16:20])
            normalise(1)
            heads_to_mix(1)
            dve.wait_ge(y_in, 32)
            for half in range(2):
                cols = slice(512 * half, 512 * (half + 1))
                for tile in range(2):
                    V.wait_full(dve)
                    n = V.emptied(v.tensor_tensor(y[:, tile, cols], psum[:, V.bank(), :], y[:, tile, cols], ALU.add))
                dve.wait_ge(*mark[f"w_out_s{half}"])
                ins = v.tensor_tensor(y[0:NS, 2, cols], mv_s[0:NS, :], y[0:NS, 2, cols], ALU.add)
                ins.then_inc(y_ready if half else wout_s, 1)
            dve.wait_ge(y_std, 1)
            v.reciprocal(stat[:, 15:18], stat[:, 12:15]).then_inc(y_rstd, 1)
            dve.wait_ge(st2_stored, 16)
            evacuate_scaled(h2_t, P, 0, range(4, 8), gain[:, 8:16])
            evacuate_scaled(h2_t, P, 1, range(4, 8), gain[:, 8:16])
            dve.wait_ge(lg_full, 1)
            dve.wait_ge(moe_zero, 2)
            dve.wait_ge(router_in, 32)
            dve.wait_ge(late_in, 16)
            v.tensor_tensor(lg[:, 0:2, :], psum[:, 4, 0:2 * E].rearrange("p (t e) -> p t e", t=2),
                            rb.unsqueeze(1).broadcast_to([P, 2, E]), ALU.add)
            link(v.tensor_tensor(lg[0:NS, 2, :], psum[0:NS, 4, 2 * E:3 * E], rb[0:NS, :], ALU.add))
            for tile in range(3):
                link(v.max(top_v[:, tile, :], lg[:, tile, :]))
            for tile in range(3):
                ins = v.max_index(top_i[:, tile, :], top_v[:, tile, :], lg[:, tile, :])
            v.tensor_tensor(top_w, top_v[:, :, 0:4], top_v[:, :, 0:1].broadcast_to([P, TILES, 4]),
                            ALU.subtract).then_inc(d4_ready, 1)
            link(ins)
            link(v.tensor_copy(top_f, top_i[:, :, 0:4]))
            hot12 = hot.rearrange("p t k e -> p (t k) e")
            hotw12 = hotw.rearrange("p t k e -> p (t k) e")
            link(v.tensor_tensor(hot12, iota[:, 0:E].unsqueeze(1).broadcast_to([P, 12, E]),
                                 top_f.rearrange("p t k -> p (t k)").unsqueeze(2).broadcast_to([P, 12, E]),
                                 ALU.is_equal))
            link(v.reduce_sum(picked, hot.rearrange("p t k e -> p t e k"), axis=AXX))
            valid = const("valid").unsqueeze(2).broadcast_to([P, TILES, E])
            link(v.tensor_tensor(picked, picked, valid, ALU.mult))
            dve.wait_ge(e4_ready, 1)
            link(v.reduce_sum(stat[:, 56:59], top_w, axis=AXX))
            link(v.reciprocal(stat[:, 59:62], stat[:, 56:59]))
            link(v.tensor_tensor(top_w, top_w, stat[:, 59:62].unsqueeze(2).broadcast_to([P, TILES, 4]), ALU.mult))
            link(v.tensor_tensor(hotw12, hot12,
                                 top_w.rearrange("p t k -> p (t k)").unsqueeze(2).broadcast_to([P, 12, E]),
                                 ALU.mult))
            link(v.reduce_sum(gates[:, :, 0:E], hotw.rearrange("p t k e -> p t e k"), axis=AXX))
            v.tensor_tensor(gates[:, :, 0:E], gates[:, :, 0:E], valid, ALU.mult).then_inc(gates_ready, 1)
            link(v.tensor_scalar(picked_off, picked, -BIG, BIG, ALU.mult, ALU.add))
            dve.wait_ge(rank_full, 1)
            v.tensor_tensor(rankm[:, :, 0:E], psum[:, 5, 0:3 * E].rearrange("p (t e) -> p t e", t=3),
                            picked_off, ALU.add).then_inc(rank_ready, 1)
            dve.wait_ge(gt_full, 1)
            v.tensor_copy(sgt[0:E, :], psum[0:E, 6, 0:TILES * P]).then_inc(sgt_ready, 1)
            tot = psum[:, 5, 3 * E:4 * E].rearrange("p (n e) -> p n e", e=2)
            link(v.reduce_max(pair_n, tot, axis=AXX))
            flat = flag.rearrange("p r n -> p (r n)")
            link(v.tensor_tensor(flag, pair_n.unsqueeze(1).broadcast_to([P, 4, PAIRS]),
                                 iota[:, SLOTS::SLOTS].unsqueeze(2).broadcast_to([P, 4, PAIRS]), ALU.is_gt))
            link(v.reduce_sum(n_over_f, flat, axis=AXX))
            v.tensor_copy(n_over_i, n_over_f).then_inc(over_ready, 1)

            def choose_bias(first):
                v.tensor_copy(esel, ident[:, bass.ds(first, 2)].unsqueeze(2).broadcast_to([P, 2, SLOTS]))\
                    .then_inc(esel_ready, 1)

            def pair(n, ahead):
                for e in range(2):
                    m = n * 2 + e
                    dve.wait_ge(gu_used, n * 16 + 8 * (e + 1))
                    u = psum[:, 0:2, :].rearrange("p b (f two) -> p b f two", two=2)
                    two = lambda w: w.rearrange("p (b f) -> p b f", b=2)
                    v.tensor_scalar(two(g_sb), u[:, :, :, 0], LIMIT, None, ALU.min).then_inc(glu_ready, 1)
                    v.tensor_scalar(two(l_sb), u[:, :, :, 1], LIMIT, -LIMIT, ALU.min, ALU.max)\
                        .then_inc(u_read, 1)
                    dve.wait_ge(glu_ready, m + 1)
                    dve.wait_ge(u_read, m + 2)
                    v.scalar_tensor_tensor(l_sb, l_sb, 1.0, g_sb, ALU.add, ALU.mult)\
                        .then_inc(lin_ready, 1)
                    dve.wait_ge(lin_ready, m + 1)
                    dve.wait_ge(sigm_ready, m + 1)
                    v.tensor_tensor(a_sb, l_sb, sg_sb, ALU.mult).then_inc(a_ready, 1)
                    if e == 0:
                        added(n)
                    elif ahead:
                        choose_bias(n * 2 + 2)

            def one_hot(n, slots, first, gated):
                dst = selg if gated else sel
                wide = [P, TILES, 2, SLOTS]
                r = rankm[:, :, bass.ds(first, 2)].unsqueeze(3).broadcast_to(wide)
                i = slots.unsqueeze(1).unsqueeze(1).broadcast_to(wide)
                if not gated:
                    v.tensor_tensor(dst, i, r, ALU.is_equal).then_inc(sel_ready, 1)
                    return
                v.tensor_tensor(dst, i, r, ALU.is_equal).then_inc(selg_eq, 1)
                dve.wait_ge(selg_eq, n + 1)
                w = gates[:, :, bass.ds(first, 2)].unsqueeze(3).broadcast_to(wide)
                v.tensor_tensor(dst, dst, w, ALU.mult).then_inc(selg_ready, 1)

            def added(n):
                for i in range(6):
                    tile, half = i // 2, i % 2
                    w = COLS[tile]
                    dve.wait_ge(comb_full, n * 6 + (i + 1))
                    dst = y[0:w, tile, 512 * half:512 * (half + 1)]
                    v.tensor_tensor(dst, psum[0:w, 3 + half, :], dst, ALU.add).then_inc(comb_added, 1)

            slots0 = iota[:, 0:SLOTS]
            dve.wait_ge(rank_ready, 1)
            one_hot(0, slots0, 0, False)
            choose_bias(0)
            with dve.Fori(0, PAIRS) as n:
                dve.wait_ge(sgt_full, n + 1)
                one_hot(n, slots0, n * 2, True)
                dve.wait_ge(x_full, n + 1)
                one_hot(n + 1, slots0, n * 2 + 2, False)
                pair(n, True)
            more = extra_pairs(dve)
            with dve.If(more > 0):
                a, b = before[0:1, 0, :], before[0:1, 1, :]
                f1 = flat[0:1, :]
                link(v.memset(b, 0.0))
                link(v.tensor_copy(b[:, 1:64], f1[:, 0:63]))
                for d in (1, 2, 4, 8, 16, 32):
                    link(v.tensor_copy(a, b))
                    link(v.tensor_tensor(a[:, d:64], b[:, d:64], b[:, 0:64 - d], ALU.add))
                    a, b = b, a
                r1, w1 = round_of[0:1, :], work[0:1]
                link(v.tensor_copy(r1.rearrange("p (r n) -> p r n", r=4),
                                   iota[0:1, SLOTS::SLOTS].unsqueeze(2).broadcast_to([1, 4, PAIRS])))
                link(v.tensor_copy(pair_of[0:1, :].rearrange("p (r n) -> p r n", r=4),
                                   iota[0:1, 0:E:2].unsqueeze(1).broadcast_to([1, 4, PAIRS])))
                for m, what in enumerate((pair_of[0:1, :], r1)):
                    link(v.tensor_tensor(w1, b.unsqueeze(1).broadcast_to([1, EXTRA, 64]),
                                         iota[0:1, 0:EXTRA].unsqueeze(2).broadcast_to([1, EXTRA, 64]),
                                         ALU.is_equal))
                    link(v.tensor_tensor(w1, w1, f1.unsqueeze(1).broadcast_to([1, EXTRA, 64]), ALU.mult))
                    link(v.tensor_tensor(w1, w1, what.unsqueeze(1).broadcast_to([1, EXTRA, 64]), ALU.mult))
                    link(v.reduce_sum(work_f[0:1, m, :], w1, axis=AXX))
                v.tensor_copy(work_i[0:1].rearrange("p a b -> p (a b)"),
                              work_f[0:1].rearrange("p a b -> p (a b)")).then_inc(work_ready, 1)
                dve.wait_ge(work_ready, 1)
                with dve.Fori(PAIRS, more + PAIRS) as n:
                    first = dve.value_load(work_i[0:1, 0, bass.ds(n - PAIRS, 1)], min_val=0, max_val=E - 2)
                    row = dve.value_load(work_i[0:1, 1, bass.ds(n - PAIRS, 1)], min_val=SLOTS,
                                         max_val=(ROUNDS - 1) * SLOTS)
                    slots = iota[:, bass.ds(row, SLOTS)]
                    dve.wait_ge(x_full, n + 1)
                    one_hot(n + 1, slots, first, False)
                    dve.wait_ge(sgt_full, n + 1)
                    one_hot(n, slots, first, True)
                    choose_bias(first)
                    pair(n, False)
            with dve.Else():
                dve.nop()
            added(more + PAIRS)
            dve.wait_ge(sq_ready, 1)
            v.reciprocal(stat[:, 53:56], stat[:, 53:56]).then_inc(f_rstd, 1)
            dve.wait_ge(f_rstd, 1)
            dve.wait_ge(fg_in, 16)
            for tile in range(3):
                w = COLS[tile]
                v.scalar_tensor_tensor(y_out[0:w, tile, :], y[0:w, tile, :], stat[0:w, 53 + tile:54 + tile],
                                       f_gain[0:w, :], ALU.mult, ALU.mult).then_inc(yo_ready, 1)

        @block.gpsimd
        def _(pool):
            g_ = nc.gpsimd
            chain = [0]

            def link(ins):
                chain[0] += 1
                ins.then_inc(pool_step, 1)
                pool.wait_ge(pool_step, chain[0])

            link(g_.memset(stat, 0.0))
            link(g_.memset(z.rearrange("p a b c -> p (a b c)"), 0.0))
            pool.sem_inc(zeroed, 1)
            link(g_.memset(q_blk.rearrange("p a b c -> p (a b c)"), 0.0))
            wait_all(pool, mark["mq_t"])
            for c in range(4):
                for u in range(2):
                    h = 2 * c + u
                    ins = g_.tensor_copy(q_blk[64 * u:64 * (u + 1), :, c, 4 * h:4 * h + 4],
                                         mq_t[64 * u:64 * (u + 1), c, LP:TOK].rearrange("p (s i) -> p s i", s=SEQS))
            ins.then_inc(qblk_ready, 1)
            def store(prompt, sampled, slot, done):
                pool.dma_start(prompt[0, 0].rearrange("(t p) h d -> p t (h d)", p=P),
                               z[:, slot, 0:2, :]).then_inc(done, 16)
                pool.dma_start(sampled[0].rearrange("s i h d -> (s i) (h d)"),
                               z[0:NS, slot, 2, :]).then_inc(done, 16)

            wait_all(pool, mark["z1"])
            store(outs[2], outs[5], 1, mk_stored)
            wait_all(pool, mark["z2"])
            g_.tensor_copy(mv_s[0:NS, :], z[0:NS, 2, 2, :]).then_inc(mvs_ready, 1)
            store(outs[3], outs[6], 2, mv_stored)
            cos, sin = (const(n).rearrange("p (t f) -> p t f", t=TILES).unsqueeze(2)
                        .broadcast_to([P, TILES, RH, 64]) for n in ("cos", "sin"))
            wait_all(pool, mark["prompt_o"])
            t1, t2 = tmp[:, :, :, 0:64], tmp[:, :, :, 64:128]
            for slot, dst, waits in ((0, rot_q, mark["z3"]), (1, rot_k, mark["z4"])):
                wait_all(pool, waits)
                src = z[:, slot].rearrange("p t (h d) -> p t h d", h=RH)
                x1, x2 = src[:, :, :, 0:64], src[:, :, :, 64:128]
                o1, o2 = dst[:, :, :, 0:64], dst[:, :, :, 64:128]
                g_.tensor_tensor(t1, x2, sin, ALU.mult)
                g_.tensor_tensor(o1, x1, cos, ALU.mult)
                g_.tensor_tensor(t2, x1, sin, ALU.mult)
                link(g_.tensor_tensor(o2, x2, cos, ALU.mult))
                g_.tensor_tensor(o1, o1, t1, ALU.subtract)
                link(g_.tensor_tensor(o2, o2, t2, ALU.add))
                pool.sem_inc(rot_done, 1)
            qd = const("q_dec").rearrange("p (t h) -> p t h", t=TILES)
            kd = const("k_dec").rearrange("p (t h) -> p t h", t=TILES)
            g_.tensor_tensor(q_dec, rot_q[:, 1:3], qd[:, 1:3].unsqueeze(3).broadcast_to([P, 2, RH, P]),
                             ALU.mult).then_inc(qdec_ready, 1)
            g_.tensor_tensor(k_dec, rot_k, kd.unsqueeze(3).broadcast_to([P, TILES, RH, P]),
                             ALU.mult).then_inc(kdec_ready, 1)
            pool.wait_ge(*mark["block6"])
            link(g_.memset(qdm_flat.rearrange("p a b -> p (a b)"), 0.0))
            pool.sem_inc(qdm_zero, 1)
            pool.wait_ge(*mark["pt3"])
            wait_all(pool, mark["z5"])
            for h in range(RH):
                if h:
                    pool.wait_ge(*mark[f"vblk{h - 1}"])
                g_.tensor_tensor(v_blk[0:NS],
                                 z[0:NS, 2, 2, h * P:(h + 1) * P].unsqueeze(1).broadcast_to([NS, SEQS, P]),
                                 const("seq_mask")[0:NS].unsqueeze(2).broadcast_to([NS, SEQS, P]),
                                 ALU.mult).then_inc(vblk_ready, 1)
            pool.wait_ge(st2_ready, 1)
            pool.dma_start(outs[4][0, 0].rearrange("h k v -> k h v"), st2).then_inc(st2_stored, 16)
            pool.wait_ge(state_new, 1)
            pool.dma_start(outs[7][0].rearrange("s h k v -> k (s h) v"),
                           state.rearrange("p s h v -> p (s h) v")).then_inc(state_stored, 16)
            pool.wait_ge(v_used, 32)
            pool.wait_ge(*mark["pt7"])
            g_.memset(bgu, 0.0)
            g_.memset(sgt, 0.0)
            g_.memset(y[:, 2, :], 0.0)
            link(g_.memset(out2, 0.0))
            pool.sem_inc(moe_zero, 1)
            pool.wait_ge(ret_ready, 1)
            pool.wait_ge(*mark["w_out"])
            g_.memset(rankm.rearrange("p a b -> p (a b)"), BIG)
            g_.memset(gates.rearrange("p a b -> p (a b)"), 0.0)
            link(g_.memset(lg.rearrange("p a b -> p (a b)"), 0.0))
            pool.sem_inc(moe_zero, 1)

        @block.sync
        def _(sp):
            sp.dma_start(page_sb[:, :], t["page_table"].rearrange("(a s) n -> a (s n)", a=1)).then_inc(pages_in, 16)
            sp.dma_start(x_sb[:, 0:2, :], x_p).then_inc(x_in, 16)
            sp.dma_start(x_sb[0:NS, 2, :], x_s).then_inc(x_in, 16)
            sp.dma_start(consts, t["shape_consts"][:, 0:ncols]).then_inc(consts_in, 16)
            sp.dma_start(gain_in[0:8, :], t["norm1_g"][0].rearrange("(k p) -> k p", p=P)).then_inc(gains_in, 16)
            sp.dma_start(gain_in[8:16, :], t["norm2_g"][0].rearrange("(k p) -> k p", p=P)).then_inc(gains_in, 16)
            sp.dma_start(gain_in[16:20, :], t["ret_norm_g"][0].rearrange("(k p) -> k p", p=P)).then_inc(gains_in, 16)

            def load_block(b):
                if b >= 3:
                    sp.wait_ge(*mark[f"block{b - 3}"])
                src = w_in[:, :, 512 * BLOCKS[b]:512 * (BLOCKS[b] + 1)] if b < 7 else \
                    w_out[:, :, 512 * (b - 7):512 * (b - 6)]
                sp.dma_start(win[:, b % 3], src).then_inc(win_in[b % 3], 16)

            def load_pages(cache, g, i, wait):
                pages = []
                for s in range(4):
                    row = page_sb[0:1, bass.ds(i * 4 + PAGES * (4 * g + s), 4)]
                    pages.append(nc.values_load_multi_w_load_instructions(
                        row, engines=[sp.engine], min_val=0, max_val=n_phys - 1)[1])
                for j in range(4):
                    wait(j)
                    for s in range(4):
                        sp.dma_start(kv[:, j, s, :], cache[bass.ds(pages[s][j], 1)].rearrange("a p n -> p (a n)"))\
                            .then_inc(kv_in[j], 16)

            def k_pages(g, i):
                load_pages(ck, g, i, lambda j: sp.wait_ge(
                    d_full, i * 8 + (mark["k_base"] + 32 * g + 2 * j - 6)))

            sp.wait_ge(pages_in, 16)
            load_block(0)
            load_block(1)
            load_pages(ck, 0, 0, lambda j: None)
            load_block(2)
            load_block(3)
            load_block(4)
            k_pages(0, 1)
            load_block(5)
            k_pages(0, 2)
            k_pages(0, 3)
            with sp.Fori(0, 4) as i:
                k_pages(1, i)
            for v in range(8):
                def wait(j, v=v):
                    if v == 0:
                        sp.wait_ge(d_full, mark["k_base"] + 64 + 2 * j - 6)
                    else:
                        sp.wait_ge(v_used, 4 * (v - 1) + j + 1)
                load_pages(cv, v // 4, v % 4, wait)
                if v == 0:
                    sp.dma_start(state.rearrange("p s h v -> p (s h) v"),
                                 t["state_ret"][0].rearrange("s h k v -> k (s h) v")).then_inc(state_in, 16)
                    load_block(6)
                if v == 2:
                    load_block(7)
                if v == 4:
                    load_block(8)

            def load_gu(e, k):
                src = w_gu[e] if isinstance(e, int) else w_gu[bass.ds(e, 1)].rearrange("a d f -> (a d) f")
                sp.dma_start(gu[:, k, :], src[P * k:P * (k + 1), :]).then_inc(gu_in[k], 16)

            def load_dn(e, q):
                src = w_dn[e] if isinstance(e, int) else w_dn[bass.ds(e, 1)].rearrange("a d f -> (a d) f")
                sp.dma_start(dn[:, 2 * q:2 * q + 2, :],
                             src[2 * P * q:2 * P * (q + 1), :].rearrange("(m p) n -> p m n", p=P))\
                    .then_inc(dn_in[q], 16)

            sp.wait_ge(*mark["block6"])
            load_gu(0, 0)
            load_gu(0, 1)
            sp.wait_ge(*mark["pt7"])
            sp.wait_ge(moe_zero, 1)
            sp.dma_start(y[:, 0:2, :], x_p).then_inc(y_in, 16)
            sp.dma_start(y[0:NS, 2, :], x_s).then_inc(y_in, 16)
            sp.dma_start(f_gain, t["final_norm_g"].partition_broadcast(P)).then_inc(fg_in, 16)
            sp.dma_start(bgu[0:E, :], t["b_gate_up"][0]).then_inc(bias_in, 16)
            sp.dma_start(out2[0:E, :], t["b_down"][0]).then_inc(bias_in, 16)
            sp.wait_ge(st2_ready, 1)
            sp.dma_start(late, t["shape_consts"][:, ncols:ncols + late_cols]).then_inc(late_in, 16)
            sp.wait_ge(state_stored, 16)
            load_gu(0, 6)
            load_gu(0, 7)
            sp.wait_ge(ret_ready, 1)
            for q in range(4):
                load_dn(0, q)
            sp.wait_ge(*mark["w_out"])
            sp.dma_start(rw, t["router_w"][0].rearrange("(k p) e -> p k e", p=P)).then_inc(router_in, 16)
            sp.dma_start(rb, t["router_b"][0:1].partition_broadcast(P).rearrange("p a e -> p (a e)"))\
                .then_inc(router_in, 16)
            for k in range(2, 6):
                load_gu(0, k)

            def load_expert(e, n, one):
                for k in range(KC):
                    sp.wait_ge(gu_used, n * 16 + (8 * one + k - 7))
                    load_gu(e, k)
                for q in range(4):
                    sp.wait_ge(dn_used, n * 8 + (4 * one + q - 3))
                    load_dn(e, q)

            load_expert(1, 0, 1)
            with sp.Fori(1, PAIRS) as n:
                for one in range(2):
                    load_expert(n * 2 + one, n, one)
            more = extra_pairs(sp)
            with sp.If(more > 0):
                sp.wait_ge(work_ready, 1)
                with sp.Fori(PAIRS, more + PAIRS) as n:
                    first = sp.value_load(work_i[0:1, 0, bass.ds(n - PAIRS, 1)], min_val=0, max_val=E - 2)
                    for one in range(2):
                        load_expert(first + one, n, one)
            with sp.Else():
                sp.nop()
            sp.wait_ge(yo_ready, 3)
            sp.dma_start(outs[0][0].rearrange("(t p) d -> p t d", p=P), y_out[:, 0:2, :]).then_inc(stored, 16)
            sp.dma_start(outs[1].rearrange("s i d -> (s i) d"), y_out[0:NS, 2, :]).then_inc(stored, 16)
            sp.wait_ge(stored, 32)
            sp.wait_ge(st2_stored, 16)
            sp.wait_ge(mk_stored, 32)
            sp.wait_ge(mv_stored, 32)
            sp.wait_ge(state_stored, 16)


_INS = ["x_prompt", "x_sample", "cache_k", "cache_v", "state_ret", "page_table", "norm1_g", "w_in",
        "ret_norm_g", "w_out", "norm2_g", "router_w", "router_b", "w_gate_up", "b_gate_up",
        "w_down", "b_down", "final_norm_g"]
_OUTS = [(1, 256, 1024), (8, 4, 1024), (1, 1, 256, 8, 64), (1, 1, 256, 8, 64), (1, 1, 4, 128, 128),
         (1, 8, 4, 8, 64), (1, 8, 4, 8, 64), (1, 8, 4, 128, 128)]


def kernel(**inputs):
    import concourse.bacc as _bacc
    from concourse.bass_utils import run_bass_kernel_spmd as _run

    nc = _bacc.Bacc("TRN2", target_bir_lowering=False, num_devices=1)
    arrays = {name: np.ascontiguousarray(inputs[name]) for name in _INS}
    table, arrays["shape_consts"] = shape_constants()
    tensors = {name: nc.dram_tensor(name, a.shape, mybir.dt.from_np(a.dtype), kind="ExternalInput").ap()
               for name, a in arrays.items()}
    outs = [nc.dram_tensor(f"out_{i}", shape, F32, kind="ExternalOutput").ap()
            for i, shape in enumerate(_OUTS)]
    build_kernel(nc, tensors, table, outs)
    r = _run(nc, [arrays], core_ids=[0])
    return tuple(r.results[0][f"out_{i}"] for i in range(len(_OUTS)))
```

```python
from contextlib import ExitStack

import numpy as np

import concourse.bass as bass
from concourse import mybir

F32 = mybir.dt.float32
I32 = mybir.dt.int32
U32 = mybir.dt.uint32
ALU = mybir.AluOpType
ACT = mybir.ActivationFunctionType
AXX = mybir.AxisListType.X

P = 128
D = 1024
KC = D // P
LP = 256
NS = 32
SEQS = 8
PAGES = 16
TILES = 3
TOK = LP + NS
COLS = (P, P, NS)
E = 32
F2 = 2048
SLOTS = 64
PAIRS = E // 2
ROUNDS = -(-TOK // SLOTS)
EXTRA = 18
BIG = 1.0e4
NEG = -1.0e30
EPS = 1e-5
RH = 4
MH = 8
SCALE = 64 ** -0.5
KSCALE = 128 ** -0.5
LIMIT = 7.0
ALPHA = 1.702
LOGITS = (4, 6, 4)
HEADS0 = (0, 2, 4, 6, 1, 3, 5, 7)
HEADS1 = (0, 2, 1, 3, 4, 6, 5, 7)
GAMMA = [1.0 - 2.0 ** (-5 - h) for h in range(RH)]


def shape_constants():
    parts = []

    def put(name, a):
        full = np.zeros((P, a.shape[1]), np.float32)
        full[: a.shape[0]] = a
        parts.append((name, full))

    put("ident", np.eye(P))
    put("eps", np.full((P, 1), EPS))
    half = 64
    inv = (np.float32(10000.0) ** (-np.arange(half, dtype=np.float32) / half)).astype(np.float32)
    pos = [np.arange(P), P + np.arange(P), PAGES * P + np.arange(NS) % 4]
    ang = [(p.astype(np.float32)[:, None] * inv[None]).astype(np.float32) for p in pos]
    for name, f in (("cos", np.cos), ("sin", np.sin)):
        t = np.zeros((P, TILES * half), np.float32)
        for n, a in enumerate(ang):
            t[: len(a), n * half:(n + 1) * half] = f(a.astype(np.float64))
        put(name, t)
    lg = np.log1p(-np.exp2(-5.0 - np.arange(RH)))
    n = np.arange(P)
    rel = n[None, :] - n[:, None]
    decay = [np.where(rel >= 0, np.exp(np.maximum(rel, 0) * g), 0.0) * KSCALE for g in lg]
    put("decay", np.concatenate(decay, 1))
    seq, step = np.arange(NS) // 4, np.arange(NS) % 4
    same = seq[:, None] == seq[None, :]
    srel = step[None, :] - step[:, None]
    put("decay_s", np.concatenate(
        [np.where(same & (srel >= 0), np.exp(np.maximum(srel, 0) * g), 0.0) * KSCALE for g in lg], 1))
    qd = np.zeros((P, TILES * RH))
    kd = np.zeros((P, TILES * RH))
    for t in range(TILES):
        m, chunk = (n, P) if t < 2 else (step, 4)
        qd[: len(m), t * RH:(t + 1) * RH] = np.exp((m[:, None] + 1.0) * lg)
        kd[: len(m), t * RH:(t + 1) * RH] = np.exp((chunk - 1.0 - m[:, None]) * lg) * KSCALE
    put("q_dec", qd)
    put("k_dec", kd)
    put("causal", np.where(n[None, :] <= n[:, None], 0.0, NEG))
    own = np.full((P, 2, NS), NEG)
    for g in range(2):
        for r in range(P):
            s, i = 4 * g + r // 32, r % 4
            own[r, g, 4 * s:4 * s + i + 1] = 0.0
    put("own_mask", own.reshape(P, -1))
    put("seq_mask", (seq[:, None] == np.arange(SEQS)[None]) * 1.0)
    valid = np.ones((P, TILES))
    valid[NS:, 2] = 0.0
    put("before8", np.tile(np.tril(np.ones((8, 8)), -1).reshape(1, 64), (P, 1)))
    put("valid", valid)
    first_late = sum(a.shape[1] for _, a in parts)
    put("iota", np.tile(np.arange(ROUNDS * SLOTS, dtype=np.float32), (P, 1)))
    put("earlier", np.triu(np.ones((P, P)), 1))
    put("ones", np.ones((P, P)))
    table, at = {"late": (first_late, 0)}, 0
    for name, a in parts:
        table[name] = (at, a.shape[1])
        at += a.shape[1]
    return table, np.ascontiguousarray(np.concatenate([a for _, a in parts], 1))


class Ring:

    def __init__(self, banks, full, empty):
        self.banks, self.full, self.empty, self.n, self.base = banks, full, empty, 0, 0

    def bank(self):
        return self.banks[self.n % 2]

    def wait_empty(self, pe):
        if self.n >= 2:
            pe.wait_ge(self.empty, self.base + (self.n - 1))

    def filled(self, instruction):
        instruction.then_inc(self.full, 1)
        self.n += 1
        return self.n

    def wait_full(self, eng):
        eng.wait_ge(self.full, self.base + (self.n + 1))

    def emptied(self, instruction):
        instruction.then_inc(self.empty, 1)
        self.n += 1
        return self.n

    def loop(self, base):
        self.base = base

    def leave(self, passes, per_pass):
        self.base = 0
        self.n += (passes - 1) * per_pass


def build_kernel(nc, t, table, outs):
    with ExitStack() as ctx:
        def sem(name):
            return ctx.enter_context(nc.semaphore(name))

        ncols = table["late"][0]
        late_cols = sum(c for _, c in table.values()) - ncols
        WORDS = 53176
        arena = ctx.enter_context(nc.sbuf_tensor("arena", [P, WORDS], F32))
        psum = ctx.enter_context(nc.psum_tensor("psum", [P, 8, 512], F32))

        def at(start, *dims):
            flat = arena[:, start:start + int(np.prod(dims))]
            if len(dims) == 1:
                return flat
            names = "abcd"[:len(dims)]
            return flat.rearrange(f"p ({' '.join(names)}) -> p {' '.join(names)}",
                                  **dict(zip(names, dims)))

        gu = at(0, KC, F2)
        win = at(0, 3, KC, 512)
        state = at(12288, SEQS, RH, P)
        DN = 16384
        dn = at(DN, KC, D)
        kt_sb = at(DN, 2, 4, 4, P)
        x_sb = at(DN + 4096, TILES, D)
        pt_prompt = at(DN, 24, P)
        s_prompt = at(DN + 4096, 24, P)
        rot_q = at(DN, TILES, RH, P)
        rot_k = at(DN + 1536, TILES, RH, P)
        rq_t = at(DN + 3072, RH, TOK)
        rk_t = at(DN + 4224, RH, TOK)
        k_dec = at(DN + 5376, TILES, RH, P)
        q_dec = at(DN + 6912, 2, RH, P)
        ret_o, sig_g = rot_q, rot_k

        C0 = DN + 8192
        consts = at(C0, ncols)

        def const(name):
            a, n = table[name]
            return consts[:, a:a + n]

        ident = const("ident")
        cur = C0 + ncols
        gain = at(cur, 20); cur += 20
        gain_in = at(cur, P); cur += P
        stat = at(cur, 64); cur += 64
        own_s = at(cur, 2, NS); cur += 2 * NS
        sm = at(cur, 2, 64); cur += 128
        pm = at(cur, 64); cur += 64
        page_sb = at(cur, SEQS * PAGES)[0:1].bitcast(I32); cur += SEQS * PAGES
        cmp = at(cur, 2, 8, 8); cur += 128
        KV = cur; cur += 8192
        kv = at(KV, 4, 4, 512)
        HT = cur; cur += 2304
        h_t = at(HT, KC, TOK)
        Z = cur; cur += 4608
        z = at(Z, 3, TILES, 512)
        mv_s = at(cur, 512); cur += 512
        SR = cur; cur += 4096
        s_raw = at(SR, 2, PAGES * P)
        Q = cur; cur += 3328
        mq_t = at(Q, 4, TOK)
        mk_t = at(Q + 1152, 4, TOK)
        q_blk = at(Q + 2304, SEQS, 4, NS)
        MX = cur; cur += 2304
        mix_t = at(MX, KC, TOK)
        o_sb = (at(SR + 1024, 512), mv_s)
        pt_sb = at(cur, 2, 512); cur += 1024
        pt_own = at(DN + 7936, 2, P)
        out_s0, out_s1 = mv_s, pt_sb[:, 0, :]
        assert cur <= WORDS, cur
        tmp = at(Q, TILES, RH, P)
        sc_p = at(Q + 1536, 2, RH, P)
        st1 = at(Q + 2560, RH, P)
        sc_s = at(Q + 3072, RH, NS)
        qdm = at(HT, RH, SEQS, 36)
        qdm_flat = at(HT, RH, 288)
        qd_t = at(HT + 1152, RH, P)
        st2 = at(HT + 1664, RH, P)
        v_blk = at(SR, SEQS, P)
        y = at(SR, TILES, D)
        f_gain = at(SR + 3072, D)
        h2_t = at(HT, KC, TOK)
        hn = at(Z, TILES, D)
        out2 = at(Z + 3072, D)
        xt = at(KV, KC, P)
        squares = at(KV + 1024, D)
        g_sb = at(KV + 2048, 512)
        l_sb = at(KV + 2560, 512)
        sg_sb = at(KV + 3072, 512)
        a_sb = at(KV + 3584, 512)
        at_sb = at(KV + 4096, 4, P)
        sel = at(KV + 4608, TILES, 2, SLOTS)
        selg = at(KV + 4992, TILES, 2, SLOTS)
        sgt = at(KV + 5376, TILES * P)
        esel = at(KV + 5760, 2, SLOTS)
        bgu = at(KV + 5888, F2)
        assert KV + 5888 + F2 <= HT
        y_out = hn
        lg = at(Q, TILES, E)
        top_v = at(Q + 96, TILES, 8)
        top_i = at(Q + 120, TILES, 8).bitcast(U32)
        top_f = at(Q + 144, TILES, 4)
        top_w = at(Q + 156, TILES, 4)
        hot = at(Q + 168, TILES, 4, E)
        hotw = at(Q + 552, TILES, 4, E)
        picked = at(Q + 936, TILES, E)
        pair_n = at(Q + 1032, PAIRS)
        flag = at(Q + 1048, 4, PAIRS)
        n_over_f = at(Q + 1112, 1)
        n_over_i = at(Q + 1113, 1).bitcast(I32)
        before = at(Q + 1114, 2, 64)
        work = at(Q + 1242, EXTRA, 64)
        work_f = at(Q + 2394, 2, EXTRA)
        work_i = at(Q + 2430, 2, EXTRA).bitcast(I32)
        pair_of = at(Q + 2466, 64)
        round_of = at(Q + 2530, 64)
        picked_off = at(Q + 2594, TILES, E)
        late = at(Q + 3328 - late_cols, late_cols)
        assert Q + 3328 - late_cols >= Q + 2690

        def late_const(name):
            a, n = table[name]
            return late[:, a - ncols:a - ncols + n]

        iota, earlier, ones = late_const("iota"), late_const("earlier"), late_const("ones")
        rw = at(C0 + table["cos"][0], KC, E)
        rb = at(C0 + table["cos"][0] + KC * E, E)
        assert (KC + 1) * E <= table["cos"][1] + table["sin"][1]
        AHEAD = 2
        gu_odd = (at(MX, F2), at(HT, F2))
        rankm = at(MX + F2, TILES, E + 2)
        gates = at(MX + F2 + TILES * (E + 2), TILES, E + 2)
        assert F2 + 2 * TILES * (E + 2) <= KC * TOK

        x_p = t["x_prompt"][0].rearrange("(t p) d -> p t d", p=P)
        x_s = t["x_sample"].rearrange("s i d -> (s i) d")
        w_in = t["w_in"][0].rearrange("(k p) e -> p k e", p=P)
        w_out = t["w_out"][0].rearrange("(k p) e -> p k e", p=P)
        w_gu = t["w_gate_up"][0]
        w_dn = t["w_down"][0]
        ck = t["cache_k"][0].rearrange("n p h d -> n p (h d)")
        cv = t["cache_v"][0].rearrange("n p h d -> n p (h d)")
        n_phys = ck.shape[0]
        BLOCKS = [4, 5, 6, 0, 1, 2, 3]
        SLOT = [0, 1, 2, 0, 1, 2, 0]

        late_in, st2_stored = sem("late_in"), sem("st2_stored")
        consts_in, tables_in, gains_in, pages_in, router_in = map(sem, (
            "consts_in", "tables_in", "gains_in", "pages_in", "router_in"))
        x_in = [sem(f"x_in{i}") for i in range(TILES)]
        win_in = [sem(f"win_in{i}") for i in range(3)]
        kv_in = [sem(f"kv_in{i}") for i in range(4)]
        kv_pool_in = [sem(f"kv_pool_in{i}") for i in range(4)]
        state_in, y_in, fg_in, bias_in = map(sem, ("state_in", "y_in", "fg_in", "bias_in"))
        a_full, a_empty, d_full, d_empty = map(sem, ("a_full", "a_empty", "d_full", "d_empty"))
        act_step, dve_step, pool_step = map(sem, ("act_step", "dve_step", "pool_step"))
        zeroed = sem("zeroed")
        x_rms, x_rstd, x_scaled, qblk_ready = map(sem, ("x_rms", "x_rstd", "x_scaled", "qblk_ready"))
        own_full, own_ready = sem("own_full"), sem("own_ready")
        qk_done, s_evac = sem("qk_done"), sem("s_evac")
        soft_bias, probs_ready, own_probs = map(sem, ("soft_bias", "probs_ready", "own_probs"))
        v_used, o_norm = sem("v_used"), sem("o_norm")
        p_bias, p_exp, p_probs = map(sem, ("p_bias", "p_exp", "p_probs"))
        mvs_ready, mk_stored, mv_stored = map(sem, ("mvs_ready", "mk_stored", "mv_stored"))
        rot_done, kdec_ready, qdec_ready, vblk_ready = map(sem, (
            "rot_done", "kdec_ready", "qdec_ready", "vblk_ready"))
        state_new, state_stored, st2_ready = map(sem, ("state_new", "state_stored", "st2_ready"))
        sig_ready, var_ready, std_ready, ret_ready = map(sem, (
            "sig_ready", "var_ready", "std_ready", "ret_ready"))
        wo_full, y_zero, y_ready, y_std, y_rstd, hn_ready = map(sem, (
            "wo_full", "y_zero", "y_ready", "y_std", "y_rstd", "hn_ready"))
        lg_full, d4_ready, e4_ready, gates_ready, rank_full = map(sem, (
            "lg_full", "d4_ready", "e4_ready", "gates_ready", "rank_full"))
        gt_full, rank_ready, moe_zero = map(sem, ("gt_full", "rank_ready", "moe_zero"))
        over_ready, work_ready = sem("over_ready"), sem("work_ready")
        gu_in = [sem(f"gu_in{i}") for i in range(KC)]
        gu_odd_in = [sem(f"gu_odd_in{i}") for i in range(AHEAD)]
        dn_in = [sem(f"dn_in{i}") for i in range(4)]
        gu_used, dn_used, u_read, esel_ready = map(sem, (
            "gu_used", "dn_used", "u_read", "esel_ready"))
        glu_ready, sigm_ready, a_ready, at_full, at_ready, out_ready = map(sem, (
            "glu_ready", "sigm_ready", "a_ready", "at_full", "at_ready", "out_ready"))
        comb_full, comb_added, sgt_full, sgt_ready = map(sem, (
            "comb_full", "comb_added", "sgt_full", "sgt_ready"))
        lin_ready, selg_eq, qdm_zero = sem("lin_ready"), sem("selg_eq"), sem("qdm_zero")
        sel_ready, selg_ready, xt_full, xt_ready = map(sem, (
            "sel_ready", "selg_ready", "xt_full", "xt_ready"))
        picked_ready = sem("picked_ready")
        sq_ready, f_rstd, yo_ready, stored = map(sem, ("sq_ready", "f_rstd", "yo_ready", "stored"))
        mark = {}

        block = ctx.enter_context(nc.Block())

        def wait_all(engine, marks):
            for semaphore, value in marks:
                engine.wait_ge(semaphore, value)

        def extra_pairs(engine):
            engine.wait_ge(over_ready, 1)
            return engine.value_load(n_over_i[0:1, 0:1], min_val=0, max_val=EXTRA)

        def load_pages(engine, seqs, done, cache, g, i, wait):
            pages = {}
            for s in seqs:
                row = page_sb[0:1, bass.ds(i * 4 + PAGES * (4 * g + s), 4)]
                pages[s] = nc.values_load_multi_w_load_instructions(
                    row, engines=[engine.engine], min_val=0, max_val=n_phys - 1)[1]
            for j in range(4):
                wait(j)
                for s in seqs:
                    engine.dma_start(kv[:, j, s, :], cache[bass.ds(pages[s][j], 1)].rearrange("a p n -> p (a n)"))\
                        .then_inc(done[j], 16)

        SP_SEQS, POOL_SEQS = (0, 1, 2), (3,)

        def k_pages(engine, seqs, done, g, i):
            load_pages(engine, seqs, done, ck, g, i, lambda j: engine.wait_ge(
                d_full, i * 8 + (mark["k_base"] + 32 * g + 2 * j - 6)))

        @block.tensor
        def _(pe):
            A = Ring((0, 1), a_full, a_empty)
            V = Ring((2, 3), d_full, d_empty)
            mm, tr = nc.tensor.matmul, nc.tensor.transpose

            def transposes(ring, blocks, rows=P):
                ring.wait_empty(pe)
                b = ring.bank()
                col = 0
                for src in blocks:
                    m = src.shape[1]
                    last = tr(psum[0:m, b, col:col + rows], src, ident[0:rows, 0:rows])
                    col += rows
                return ring.filled(last)

            def project(b, after_first=lambda: None):
                w = win[:, b % 3]
                pe.wait_ge(win_in[b % 3], 16 * (b // 3 + 1))
                lhs = h_t
                marks = []
                for tile, ring in ((0, A), (1, V)):
                    ring.wait_empty(pe)
                    for k in range(KC):
                        last = mm(psum[:, ring.bank(), :], lhs[:, k, tile * P:(tile + 1) * P],
                                  w[:, k, :], start=k == 0, stop=k == KC - 1)
                    marks.append((ring, ring.filled(last)))
                    if tile == 0:
                        after_first()
                ring = V if b % 2 else A
                ring.wait_empty(pe)
                for k in range(KC):
                    for j in range(4):
                        last = mm(psum[NS * j:NS * (j + 1), ring.bank(), 0:P],
                                  lhs[:, k, LP:TOK], w[:, k, j * P:(j + 1) * P],
                                  start=k == 0, stop=k == KC - 1)
                marks.append((ring, ring.filled(last)))
                mark[f"block{b}"] = (ring.full, ring.n)
                mark[f"z{b}"] = [(r.empty, n) for r, n in marks]
                return marks

            def evacuated(marks):
                for ring, n in marks:
                    pe.wait_ge(ring.empty, n)

            def z_transposes(slot, sample_ring, before=()):
                got = []
                for tile, ring in ((0, A), (1, V), (2, sample_ring)):
                    r = COLS[tile]
                    n = transposes(ring, [z[0:r, slot, tile, c * P:(c + 1) * P] for c in range(4)], r)
                    got.append((ring, n))
                return got

            pe.sem_inc(qk_done, 2)
            pe.sem_inc(s_evac, 1)
            pe.sem_inc(u_read, 1)
            pe.wait_ge(consts_in, 16)
            pe.wait_ge(gains_in, 48)
            transposes(V, [gain_in[0:20, :]], 20)
            for tile in range(2):
                pe.wait_ge(x_in[tile], 16)
                for ring, k0 in ((A, 0), (V, 4)):
                    n = transposes(ring, [x_sb[:, tile, k * P:(k + 1) * P] for k in range(k0, k0 + 4)])
            pe.wait_ge(x_scaled, 1)
            n_x = transposes(A, [x_sb[0:NS, 2, k * P:(k + 1) * P] for k in range(KC)], NS)
            pe.wait_ge(a_empty, n_x)
            pe.wait_ge(d_empty, V.n)
            mq = project(0)
            mk = project(1)
            evacuated(mq)
            mqt = z_transposes(0, A)
            evacuated(mk)
            mark["mq_t"] = [(r.empty, n) for r, n in mqt]
            mkt = z_transposes(1, V)
            mv = project(2)
            pe.wait_ge(qblk_ready, 1)
            evacuated(mkt)
            for g in range(2):
                for c in range(4):
                    for s in range(4):
                        last = mm(psum[NS * s:NS * (s + 1), 5, NS * g:NS * (g + 1)],
                                  q_blk[:, 4 * g + s, c, :], mk_t[:, c, LP:TOK],
                                  start=c == 0, stop=c == 3)
            last.then_inc(own_full, 1)

            mark["k_base"] = V.n
            for g in range(2):
                a0, v0 = A.n, V.n
                with pe.Fori(0, 4) as i:
                    A.loop(i * 8)
                    V.loop(i * 8)

                    def scores(j):
                        pe.wait_ge(a_empty, i * 8 + (a0 + 2 * j + 2))
                        pe.wait_ge(d_empty, i * 8 + (v0 + 2 * j + 2))
                        if j == 0:
                            pe.wait_ge(s_evac, i + (4 * g + 1))
                        for c in range(4):
                            for s in range(4):
                                last = mm(psum[NS * s:NS * (s + 1), 4, P * j:P * (j + 1)],
                                          q_blk[:, 4 * g + s, c, :], kt_sb[:, j % 2, s, c, :],
                                          start=c == 0, stop=c == 3)
                        last.then_inc(qk_done, 1)

                    for j in range(4):
                        pe.wait_ge(kv_in[j], i * 48 + 48 * (4 * g + 1))
                        pe.wait_ge(kv_pool_in[j], i * 16 + 16 * (4 * g + 1))
                        for s in range(4):
                            transposes(A if s < 2 else V,
                                       [kv[:, j, s, c * P:(c + 1) * P] for c in range(4)])
                        if j:
                            scores(j - 1)
                    scores(3)
                A.leave(4, 8)
                V.leave(4, 8)

            def p_transposes(v):
                g, q = v // 4, v % 4
                pe.wait_ge(probs_ready, g + 1)
                n = transposes(A, [s_raw[:, g, (4 * q + j) * P:(4 * q + j + 1) * P] for j in range(4)])
                mark[f"pt{v}"] = (a_full, n)
                return n

            def own_transposes(g):
                pe.wait_ge(own_probs, g + 1)
                V.wait_empty(pe)
                return V.filled(tr(psum[0:NS, V.bank(), 0:P], own_s[:, g, :], ident))

            def values(v, n_pt, n_own=None):
                g, q = v // 4, v % 4
                pe.wait_ge(a_empty, n_pt)
                if q == 0:
                    pe.wait_ge(d_empty, n_own)
                    pe.wait_ge(mvs_ready, 1)
                    for s in range(4):
                        mm(psum[NS * s:NS * (s + 1), 6 + g, :], pt_own[0:NS, g, NS * s:NS * (s + 1)],
                           mv_s[0:NS, :], start=True, stop=False, skip_group_check=True)
                for j in range(4):
                    pe.wait_ge(kv_in[j], 48 * 8 + 64 * (v + 1))
                    for s in range(4):
                        last = mm(psum[NS * s:NS * (s + 1), 6 + g, :],
                                  pt_sb[:, v % 2, j * P + NS * s:j * P + NS * (s + 1)],
                                  kv[:, j, s, :], start=False, stop=q == 3 and j == 3,
                                  skip_group_check=True)
                    last.then_inc(v_used, 1)

            def o_transposes(g):
                pe.wait_ge(o_norm, g + 1)
                n = transposes(V, [o_sb[g][:, c * P:(c + 1) * P] for c in range(4)])
                mark[f"o_t{g}"] = (d_full, n)

            project(3)
            pt = p_transposes(0)
            po = own_transposes(0)
            for u in range(6):
                V.wait_empty(pe)
                heads = HEADS0[4 * u:4 * u + 4] if u < 2 else HEADS1[2 * (u - 2):2 * (u - 2) + 2]
                for n, h in enumerate(heads):
                    r = 64 * (h % 2)
                    tile, w = (0, P) if u < 2 else (1, LP)
                    last = mm(psum[:, V.bank(), n * w:(n + 1) * w],
                              mq_t[r:r + 64, h // 2, tile * P:(tile + 1) * P],
                              mk_t[r:r + 64, h // 2, 0:w], start=True, stop=True)
                V.filled(last)
            values(0, pt, po)
            pt = p_transposes(1)
            project(4, lambda: values(1, pt))
            pt = p_transposes(2)
            pe.wait_ge(p_probs, 1)
            for u in range(6):
                n = transposes(V if u % 2 else A, [s_prompt[:, 4 * u + j, :] for j in range(4)])
            pe.wait_ge(a_empty, A.n)
            pe.wait_ge(d_empty, V.n)
            evacuated(mv)
            for half, ring in ((0, A), (1, V)):
                ring.wait_empty(pe)
                b = ring.bank()
                for c in range(2):
                    for u in range(2):
                        h = 2 * (2 * half + c) + u
                        o = psum[64 * u:64 * (u + 1), b, c * LP:(c + 1) * LP]
                        n0, n1 = HEADS0.index(h), 8 + 2 * HEADS1.index(h)
                        mm(o[:, 0:P], z[:, 2, 0, 64 * h:64 * (h + 1)], pt_prompt[:, n0, :],
                           start=True, stop=True)
                        mm(o[:, P:LP], z[:, 2, 0, 64 * h:64 * (h + 1)], pt_prompt[:, n1, :],
                           start=True, stop=False)
                        last = mm(o[:, P:LP], z[:, 2, 1, 64 * h:64 * (h + 1)],
                                  pt_prompt[:, n1 + 1, :], start=False, stop=True)
                ring.filled(last)
            mark["prompt_o"] = [(A.full, A.n), (V.full, V.n)]
            prompt_mix = [(A, A.n), (V, V.n)]
            values(2, pt)
            pt = p_transposes(3)
            rv = project(5)
            values(3, pt)
            pt = p_transposes(4)
            po = own_transposes(1)
            project(6, lambda: values(4, pt, po))
            o_transposes(0)
            pe.wait_ge(rot_done, 2)
            rt = []
            for src, sample_ring in ((rot_q, A), (rot_k, V)):
                for tile, ring in ((0, A), (1, V), (2, sample_ring)):
                    r = COLS[tile]
                    rt.append((ring, transposes(ring, [src[0:r, tile, c, :] for c in range(4)], r)))
            pe.wait_ge(qdec_ready, 1)
            rt.append((A, transposes(A, [q_dec[:, 0, c, :] for c in range(4)])))
            rt.append((V, transposes(V, [q_dec[0:NS, 1, c, :] for c in range(4)], NS)))
            mark["ret_t"] = [(A.full, A.n), (V.full, V.n)]
            pt = p_transposes(5)
            values(5, pt)
            evacuated(rt)
            sc = []
            for tile in range(3):
                w = COLS[tile]
                lo = tile * P
                V.wait_empty(pe)
                for h in range(RH):
                    last = mm(psum[0:w, V.bank(), h * w:(h + 1) * w], rk_t[:, h, lo:lo + w],
                              rq_t[:, h, lo:lo + w], start=True, stop=True)
                sc.append(V.filled(last))
            pe.wait_ge(kdec_ready, 1)
            evacuated(rv)
            for tile, ring in ((0, A), (1, V)):
                ring.wait_empty(pe)
                for h in range(RH):
                    last = mm(psum[:, ring.bank(), h * P:(h + 1) * P], k_dec[:, tile, h, :],
                              z[:, 2, tile, h * P:(h + 1) * P], start=True, stop=True)
                n = ring.filled(last)
                if tile == 0:
                    n_st1 = n
                    mark["st1"] = (a_empty, n)

            def output_part(tile, half, bank, chunks):
                for k in chunks:
                    last = mm(psum[:, bank, :], mix_t[:, k, tile * P:(tile + 1) * P],
                              win[:, (7 + half) % 3, k, :], start=k == 4, stop=k == 3,
                              skip_group_check=True)
                return last

            def output_sample(half):
                A.wait_empty(pe)
                for k in range(KC):
                    for j in range(4):
                        last = mm(psum[NS * j:NS * (j + 1), A.bank(), 0:P], mix_t[:, k, LP:TOK],
                                  win[:, (7 + half) % 3, k, j * P:(j + 1) * P],
                                  start=k == 0, stop=k == KC - 1)
                mark[f"w_out_s{half}"] = (a_empty, A.filled(last))

            def retention_output(tile):
                A.wait_empty(pe)
                for h in range(RH):
                    o = psum[:, A.bank(), h * P:(h + 1) * P]
                    last = mm(o, sc_p[:, tile, h, :], z[:, 2, tile, h * P:(h + 1) * P],
                              start=True, stop=tile == 0, skip_group_check=True)
                    if tile == 1:
                        last = mm(o, qd_t[:, h, :], st1[:, h, :], start=False, stop=True,
                                  skip_group_check=True)
                mark["ret_out"] = (a_empty, A.filled(last))

            def sample_retention_output():
                A.wait_empty(pe)
                o = [psum[NS * h:NS * (h + 1), A.bank(), 0:P] for h in range(RH)]
                for h in range(RH):
                    mm(o[h], sc_s[0:NS, h, :], z[0:NS, 2, 2, h * P:(h + 1) * P],
                       start=True, stop=False, skip_group_check=True)
                for s in range(SEQS):
                    for h in range(RH):
                        last = mm(o[h], qdm_flat[:, h, NS * s:NS * (s + 1)], state[:, s, h, :],
                                  start=False, stop=s == SEQS - 1, skip_group_check=True)
                A.filled(last)

            pe.wait_ge(d_empty, sc[2])
            pe.wait_ge(state_in, 16)
            sample_retention_output()

            def sample_state(h):
                pe.wait_ge(vblk_ready, h + 1)
                for half in range(2):
                    V.wait_empty(pe)
                    last = mm(psum[:, V.bank(), :], k_dec[0:NS, 2, h, :],
                              v_blk[0:NS, 4 * half:4 * half + 4, :], start=True, stop=True)
                    V.filled(last)
                mark[f"vblk{h}"] = (V.full, V.n)

            attention, retention = range(4, 8), range(4)
            pe.wait_ge(s_evac, 9)
            evacuated(prompt_mix)
            pe.wait_ge(win_in[1], 16 * 3)
            sample_state(0)
            pt = p_transposes(6)
            values(6, pt)
            sample_state(1)
            output_part(0, 0, 4, attention)
            pe.wait_ge(a_empty, n_st1)
            retention_output(0)
            retention_output(1)
            pe.wait_ge(own_ready, 1)
            output_part(1, 0, 5, attention)
            sample_state(2)
            pe.wait_ge(o_norm, 1)
            pe.wait_ge(win_in[2], 16 * 3)
            output_part(0, 1, 6, attention)
            sample_state(3)
            pt = p_transposes(7)
            values(7, pt)
            pe.wait_ge(ret_ready, 1)
            ret_mix = []
            for tile, ring in ((0, A), (1, V), (2, A)):
                r = COLS[tile]
                ret_mix.append((ring, transposes(ring, [tmp[0:r, tile, c, :] for c in range(4)], r)))
            mark["ret_mix"] = [(r.full, n) for r, n in ret_mix]
            o_transposes(1)
            def logits(tile):
                w = COLS[tile]
                for k in range(KC):
                    last = mm(psum[0:w, LOGITS[tile], E * tile:E * (tile + 1)], h2_t[:, k, tile * P:tile * P + w],
                              rw[:, k, :], start=k == 0, stop=k == KC - 1)
                return last

            def norm_transposes(tile):
                for ring, k0 in ((A, 0), (V, 4)):
                    transposes(ring, [hn[:, tile, k * P:(k + 1) * P] for k in range(k0, k0 + 4)])

            evacuated(ret_mix[:1])
            output_part(0, 0, 4, retention).then_inc(wo_full, 1)
            output_part(0, 1, 6, retention).then_inc(wo_full, 1)
            pe.wait_ge(a_empty, A.n)
            pe.wait_ge(d_empty, V.n)
            output_sample(0)
            output_sample(1)
            output_part(1, 0, 5, retention).then_inc(wo_full, 1)
            output_part(1, 1, 7, attention)
            pe.wait_ge(hn_ready, 1)
            norm_transposes(0)
            pe.wait_ge(hn_ready, 2)
            transposes(A, [hn[0:NS, 2, k * P:(k + 1) * P] for k in range(KC)], NS)
            output_part(1, 1, 7, retention).then_inc(wo_full, 1)
            mark["w_out"] = (wo_full, 4)

            pe.wait_ge(a_empty, A.n)
            pe.wait_ge(d_empty, V.n)
            pe.wait_ge(router_in, 32)
            logits(0)
            logits(2).then_inc(lg_full, 1)
            pe.wait_ge(hn_ready, 3)
            norm_transposes(1)
            pe.wait_ge(a_empty, A.n)
            pe.wait_ge(d_empty, V.n)
            logits(1).then_inc(lg_full, 1)
            pe.wait_ge(late_in, 16)
            def count(tile, lhs, src, **flags):
                return mm(psum[:, 5, E * tile:E * (tile + 1)], lhs, picked[:, src, :],
                          skip_group_check=True, **flags)

            pe.wait_ge(picked_ready, 2)
            count(0, earlier, 0, start=True, stop=True)
            count(1, ones, 0, start=False, stop=False)
            count(2, ones, 0, start=False, stop=False)
            count(2, earlier, 2, start=False, stop=False)
            pe.wait_ge(picked_ready, 3)
            count(1, earlier, 1, start=False, stop=True)
            count(2, ones, 1, start=False, stop=True).then_inc(rank_full, 1)

            def gather(n):
                pe.wait_ge(sel_ready, n + 1)
                for k in range(KC):
                    for tile in range(3):
                        last = mm(psum[:, 6 + k // 4, P * (k % 4):P * (k % 4 + 1)],
                                  hn[:, tile, k * P:(k + 1) * P],
                                  sel[:, tile].rearrange("p a b -> p (a b)"),
                                  start=tile == 0, stop=tile == 2)
                last.then_inc(xt_full, 1)

            def combine(m):
                pe.wait_ge(sgt_ready, m + 1)
                pe.wait_ge(out_ready, m * 2 + 1)
                for u in range(6):
                    tile, half = u // 2, u % 2
                    if u >= 2:
                        pe.wait_ge(comb_added, m * 6 + (u - 1))
                    w = COLS[tile]
                    mm(psum[0:w, 3 + half, :], sgt[:, P * tile:P * tile + w],
                       out2[:, 512 * half:512 * (half + 1)], start=True, stop=True)\
                        .then_inc(comb_full, 1)

            def pair(n, ahead):
                pe.wait_ge(xt_ready, n + (1 if ahead else 2))
                pe.wait_ge(esel_ready, n + (1 if ahead else 2))
                for e in range(2):
                    pe.wait_ge(u_read, n * 2 + (e + 1))
                    lhs = slice(SLOTS * e, SLOTS * (e + 1))
                    for b in range(2):
                        for g in range(2):
                            c = 1024 * g + 512 * b
                            mm(psum[64 * g:64 * (g + 1), b, :], esel[:, e, :], bgu[:, c:c + 512],
                               start=True, stop=False, skip_group_check=True)
                    for k in range(KC):
                        if k >= AHEAD:
                            pe.wait_ge(gu_in[k], n * 32 + 16 * (e + 1))
                        else:
                            pe.wait_ge((gu_odd_in if e else gu_in)[k], n * 16 + 16)
                        w = gu_odd[k] if e and k < AHEAD else gu[:, k, :]
                        for b in range(2):
                            for g in range(2):
                                c = 1024 * g + 512 * b
                                last = mm(psum[64 * g:64 * (g + 1), b, :], xt[:, k, lhs],
                                          w[:, c:c + 512], start=False, stop=k == KC - 1,
                                          skip_group_check=True)
                        last.then_inc(gu_used, 1)
                    if e == 0:
                        combine(n)
                        pe.wait_ge(selg_ready, n + 1)
                        for tile in range(3):
                            last = tr(psum[:, 7, P * tile:P * (tile + 1)],
                                      selg[:, tile].rearrange("p a b -> p (a b)"), ident)
                        last.then_inc(sgt_full, 1)
                    elif ahead:
                        pe.wait_ge(sgt_ready, n + 2)
                        gather(n + 1)
                    pe.wait_ge(a_ready, n * 2 + (e + 1))
                    for q in range(4):
                        last = tr(psum[:, 5, P * q:P * (q + 1)], a_sb[:, P * q:P * (q + 1)], ident)
                    last.then_inc(at_full, 1)
                    if e == 1:
                        pe.wait_ge(comb_added, n * 6 + 6)
                    pe.wait_ge(at_ready, n * 2 + (e + 1))
                    pe.wait_ge(out_ready, n * 2 + (e + 1))
                    for m in range(KC):
                        if m % 2 == 0:
                            pe.wait_ge(dn_in[m // 2], n * 32 + 16 * (e + 1))
                        half, q = m // 4, m % 4
                        for g in range(2):
                            last = mm(psum[64 * g:64 * (g + 1), 2, :],
                                      at_sb[:, q, SLOTS * half:SLOTS * (half + 1)],
                                      dn[:, m, 512 * g:512 * (g + 1)],
                                      start=m == 0, stop=m == KC - 1)
                        if m % 2:
                            last.then_inc(dn_used, 1)

            gather(0)
            for tile in range(TILES):
                last = count(3, ones, tile, start=tile == 0, stop=tile == TILES - 1)
            last.then_inc(rank_full, 1)
            pe.wait_ge(gates_ready, 1)
            for tile in range(3):
                last = tr(psum[0:E, 2, P * tile:P * (tile + 1)], gates[:, tile, 0:E], ident)
            last.then_inc(gt_full, 1)
            pe.wait_ge(bias_in, 32)
            pe.sem_inc(out_ready, 1)
            pe.sem_inc(sgt_full, 1)
            with pe.Fori(0, PAIRS) as n:
                pair(n, True)
            more = extra_pairs(pe)
            with pe.If(more > 0):
                with pe.Fori(PAIRS, more + PAIRS) as n:
                    pe.wait_ge(xt_ready, n + 1)
                    pe.wait_ge(sgt_ready, n + 1)
                    gather(n + 1)
                    pair(n, False)
            with pe.Else():
                pe.nop()
            combine(more + PAIRS)

        @block.scalar
        def _(act):
            A = Ring((0, 1), a_full, a_empty)
            chain = [0]

            def link(ins):
                chain[0] += 1
                ins.then_inc(act_step, 1)
                act.wait_ge(act_step, chain[0])

            def copy(out, in_, scale=1.0):
                return nc.scalar.activation(out, in_, ACT.Copy, scale=scale)

            def evacuate(out, rows=P, width=512):
                A.wait_full(act)
                A.emptied(copy(out, psum[0:rows, A.bank(), 0:width]))

            def evacuate_sample(out):
                A.wait_full(act)
                for j in range(4):
                    ins = copy(out[:, P * j:P * (j + 1)], psum[NS * j:NS * (j + 1), A.bank(), 0:P])
                A.emptied(ins)

            def evacuate_scaled(dst, w, tile, chunks, gains):
                A.wait_full(act)
                for n, k in enumerate(chunks):
                    ins = copy(dst[:, k, tile * P:tile * P + w],
                               psum[:, A.bank(), n * w:(n + 1) * w], scale=gains[:, k:k + 1])
                A.emptied(ins)

            def evacuate_t(dst, tile):
                w = COLS[tile]
                A.wait_full(act)
                A.emptied(copy(dst[:, 0:4, tile * P:tile * P + w],
                               psum[:, A.bank(), 0:4 * w].rearrange("p (c w) -> p c w", c=4)))

            act.wait_ge(zeroed, 1)
            act.wait_ge(consts_in, 16)

            def square(tile):
                r = COLS[tile]
                act.wait_ge(x_in[tile], 16)
                link(nc.scalar.activation(at(MX, D)[0:r], x_sb[0:r, tile, :], ACT.Square,
                                          accum_out=stat[0:r, tile:tile + 1]))

            def square_root(tiles):
                nc.scalar.activation(stat[:, 3 + tiles.start:3 + tiles.stop], stat[:, tiles], ACT.Sqrt,
                                     scale=1.0 / D, bias=const("eps")).then_inc(x_rms, 1)

            square(2)
            square_root(slice(2, 3))
            act.wait_ge(x_rstd, 1)
            copy(x_sb[0:NS, 2, :], x_sb[0:NS, 2, :], scale=stat[0:NS, 8:9]).then_inc(x_scaled, 1)
            act.wait_ge(d_empty, 1)
            evacuate_scaled(h_t, P, 0, range(4), gain)
            evacuate_scaled(h_t, P, 1, range(4), gain)
            evacuate_scaled(h_t, NS, 2, range(KC), gain)
            square(0)
            square(1)
            square_root(slice(0, 2))
            act.wait_ge(x_rstd, 2)
            act.wait_ge(zeroed, 2)

            def evacuate_block(slot):
                A.wait_full(act)
                A.emptied(copy(z[:, slot, 0, :], psum[:, A.bank(), :], scale=stat[:, 6:7]))

            evacuate_block(0)
            evacuate_sample(z[0:NS, 0, 2, :])
            evacuate_block(1)
            evacuate_t(mq_t, 0)
            evacuate_t(mq_t, 2)
            evacuate_t(mk_t, 0)
            evacuate_block(2)
            evacuate_sample(z[0:NS, 2, 2, :])

            for g in range(2):
                with act.Fori(0, 4) as i:
                    A.loop(i * 8)
                    for j in range(4):
                        for s in range(2):
                            if s == 0:
                                act.wait_ge(qk_done, i * 4 + (16 * g + j + 1))
                            evacuate(kt_sb[:, j % 2, s].rearrange("p c t -> p (c t)"))
                    act.wait_ge(qk_done, i * 4 + (16 * g + 4 + 2))
                    copy(s_raw[:, g, bass.ds(i * 512, 512)], psum[:, 4, :]).then_inc(s_evac, 1)
                A.leave(4, 8)

            def probabilities(g):
                act.wait_ge(soft_bias, g + 1)
                for b in range(8):
                    s = s_raw[:, g, 256 * b:256 * (b + 1)]
                    ins = nc.scalar.activation(s, s, ACT.Exp, bias=sm[:, g, 24 + b:25 + b],
                                               scale=SCALE, accum_out=sm[:, g, 40 + b:41 + b])
                ins.then_inc(probs_ready, 1)
                nc.scalar.activation(own_s[:, g, :], own_s[:, g, :], ACT.Exp,
                                     bias=sm[:, g, 32:33], scale=SCALE,
                                     accum_out=sm[:, g, 48:49]).then_inc(own_probs, 1)

            def evacuate_pt(v):
                if v >= 2:
                    act.wait_ge(v_used, 4 * (v - 1))
                evacuate(pt_sb[:, v % 2, :])

            probabilities(0)
            evacuate_block(0)
            evacuate_pt(0)
            act.wait_ge(p_bias, 1)
            for b in range(MH):
                ins = nc.scalar.activation(s_prompt[:, b, :], s_prompt[:, b, :], ACT.Exp,
                                           bias=pm[:, 16 + b:17 + b], scale=SCALE,
                                           accum_out=pm[:, 32 + b:33 + b])
            for h in range(MH):
                s = s_prompt[:, 8 + 2 * h:10 + 2 * h, :]
                ins = nc.scalar.activation(s, s, ACT.Exp, bias=pm[:, 24 + h:25 + h], scale=SCALE,
                                           accum_out=pm[:, 40 + h:41 + h])
            ins.then_inc(p_exp, 1)
            evacuate_pt(1)
            act.wait_ge(mk_stored, 32)
            evacuate_block(1)
            evacuate_sample(z[0:NS, 1, 2, :])
            evacuate_pt(2)
            for u in range(0, 6, 2):
                evacuate(pt_prompt[:, 4 * u:4 * u + 4, :].rearrange("p b t -> p (b t)"))
            A.wait_full(act)
            A.emptied(copy(mix_t[:, 4:6, 0:LP], psum[:, A.bank(), :].rearrange("p (c w) -> p c w", c=2)))
            evacuate_pt(3)
            act.wait_ge(mv_stored, 32)
            act.wait_ge(mvs_ready, 1)
            evacuate_block(2)
            probabilities(1)
            evacuate_pt(4)
            act.wait_ge(rot_done, 1)
            evacuate_block(0)
            evacuate_sample(z[0:NS, 0, 2, :])
            evacuate_t(rq_t, 0)
            evacuate_t(rq_t, 2)
            evacuate_t(rk_t, 0)
            evacuate(qd_t.rearrange("p h t -> p (h t)"))
            evacuate_pt(5)
            evacuate(st1.rearrange("p h t -> p (h t)"))
            act.wait_ge(qdec_ready, 1)
            act.wait_ge(kdec_ready, 1)

            evacuate_sample(ret_o[0:NS, 2].rearrange("p h d -> p (h d)"))
            evacuate_pt(6)
            evacuate(ret_o[:, 0].rearrange("p h d -> p (h d)"))
            evacuate(ret_o[:, 1].rearrange("p h d -> p (h d)"))
            wait_all(act, mark["z6"])
            nc.scalar.activation(sig_g, z[:, 0].rearrange("p t (h d) -> p t h d", h=RH),
                                 ACT.Sigmoid).then_inc(sig_ready, 1)
            act.wait_ge(var_ready, 1)
            nc.scalar.activation(stat[:, 36:48], stat[:, 24:36], ACT.Sqrt, scale=1.0 / P,
                                 bias=const("eps")).then_inc(std_ready, 1)
            evacuate_pt(7)
            evacuate_scaled(mix_t, P, 0, range(4), gain[:, 16:20])
            evacuate_scaled(mix_t, NS, 2, range(4), gain[:, 16:20])

            def root(n, tile):
                act.wait_ge(y_ready, n + 1)
                link(nc.scalar.activation(squares, y[:, tile, :], ACT.Square,
                                          accum_out=stat[:, 9 + tile:10 + tile]))
                nc.scalar.activation(stat[:, 12 + tile:13 + tile], stat[:, 9 + tile:10 + tile], ACT.Sqrt,
                                     scale=1.0 / D, bias=const("eps")).then_inc(y_std, 1)

            def scaled(n, tile):
                act.wait_ge(y_rstd, n + 1)
                copy(hn[:, tile, :], y[:, tile, :], scale=stat[:, 15 + tile:16 + tile])\
                    .then_inc(hn_ready, 1)

            root(0, 0)
            evacuate_sample(out_s0[0:NS, :])
            evacuate_sample(out_s1[0:NS, :])
            scaled(0, 0)
            root(1, 2)
            scaled(1, 2)
            act.wait_ge(st2_stored, 16)
            evacuate_scaled(h2_t, P, 0, range(4), gain[:, 8:16])
            evacuate_scaled(h2_t, NS, 2, range(KC), gain[:, 8:16])
            root(2, 1)
            scaled(2, 1)
            evacuate_scaled(h2_t, P, 1, range(4), gain[:, 8:16])
            act.wait_ge(d4_ready, 1)
            nc.scalar.activation(top_w, top_w, ACT.Exp).then_inc(e4_ready, 1)

            def gathered(n):
                act.wait_ge(xt_full, n + 1)
                for k in range(KC):
                    ins = copy(xt[:, k, :], psum[:, 6 + k // 4, P * (k % 4):P * (k % 4 + 1)],
                               scale=gain[:, 8 + k:9 + k])
                ins.then_inc(xt_ready, 1)

            def pair(n, ahead):
                for e in range(2):
                    act.wait_ge(glu_ready, n * 2 + (e + 1))
                    nc.scalar.activation(sg_sb, g_sb, ACT.Sigmoid, scale=ALPHA).then_inc(sigm_ready, 1)
                    if e == 0:
                        act.wait_ge(sgt_full, n + 2)
                        copy(sgt, psum[:, 7, 0:TILES * P]).then_inc(sgt_ready, 1)
                    act.wait_ge(at_full, n * 2 + (e + 1))
                    copy(at_sb.rearrange("p q t -> p (q t)"), psum[:, 5, :]).then_inc(at_ready, 1)
                    if e == 1 and ahead:
                        gathered(n + 1)
                    act.wait_ge(dn_used, n * 8 + 4 * (e + 1))
                    for g in range(2):
                        ins = copy(out2[64 * e:64 * (e + 1), 512 * g:512 * (g + 1)],
                                   psum[64 * g:64 * (g + 1), 2, :])
                    ins.then_inc(out_ready, 1)

            gathered(0)
            with act.Fori(0, PAIRS) as n:
                pair(n, True)
            more = extra_pairs(act)
            with act.If(more > 0):
                with act.Fori(PAIRS, more + PAIRS) as n:
                    gathered(n + 1)
                    pair(n, False)
            with act.Else():
                act.nop()
            for tile in range(3):
                act.wait_ge(comb_added, more * 6 + (6 * PAIRS + 2 * (tile + 1)))
                link(nc.scalar.activation(squares, y[:, tile, :], ACT.Square,
                                          accum_out=stat[:, 50 + tile:51 + tile]))
                nc.scalar.activation(stat[:, 53 + tile:54 + tile], stat[:, 50 + tile:51 + tile], ACT.Sqrt,
                                     scale=1.0 / D, bias=const("eps")).then_inc(sq_ready, 1)

        @block.vector
        def _(dve):
            V = Ring((2, 3), d_full, d_empty)
            v = nc.vector
            chain = [0]

            def link(ins):
                chain[0] += 1
                ins.then_inc(dve_step, 1)
                dve.wait_ge(dve_step, chain[0])

            def evacuate(out, rows=P, width=512):
                V.wait_full(dve)
                V.emptied(v.tensor_copy(out, psum[0:rows, V.bank(), 0:width]))

            def evacuate_sample(out):
                V.wait_full(dve)
                for j in range(4):
                    ins = v.tensor_copy(out[:, P * j:P * (j + 1)], psum[NS * j:NS * (j + 1), V.bank(), 0:P])
                V.emptied(ins)

            def evacuate_scaled(dst, w, tile, chunks, gains):
                V.wait_full(dve)
                for n, k in enumerate(chunks):
                    ins = v.tensor_scalar(dst[:, k, tile * P:tile * P + w],
                                          psum[:, V.bank(), n * w:(n + 1) * w],
                                          gains[:, k:k + 1], None, ALU.mult)
                V.emptied(ins)

            def evacuate_t(dst, tile):
                w = COLS[tile]
                V.wait_full(dve)
                V.emptied(v.tensor_copy(dst[:, 0:4, tile * P:tile * P + w],
                                        psum[:, V.bank(), 0:4 * w].rearrange("p (c w) -> p c w", c=4)))

            evacuate(gain, width=20)
            dve.wait_ge(x_rms, 1)
            v.reciprocal(stat[:, 8:9], stat[:, 5:6]).then_inc(x_rstd, 1)
            dve.wait_ge(d_empty, 1)
            evacuate_scaled(h_t, P, 0, range(4, 8), gain)
            evacuate_scaled(h_t, P, 1, range(4, 8), gain)
            dve.wait_ge(x_rms, 2)
            v.reciprocal(stat[:, 6:8], stat[:, 3:5]).then_inc(x_rstd, 1)
            dve.wait_ge(x_rstd, 2)
            dve.wait_ge(zeroed, 2)

            def evacuate_block(slot):
                V.wait_full(dve)
                V.emptied(v.tensor_scalar(z[:, slot, 1, :], psum[:, V.bank(), :], stat[:, 7:8], None,
                                          ALU.mult))

            evacuate_block(0)
            evacuate_block(1)
            evacuate_sample(z[0:NS, 1, 2, :])
            evacuate_t(mq_t, 1)
            evacuate_t(mk_t, 1)
            evacuate_t(mk_t, 2)
            evacuate_block(2)
            dve.wait_ge(own_full, 1)
            dve.wait_ge(tables_in, 16)
            v.tensor_tensor(own_s.rearrange("p g t -> p (g t)"), psum[:, 5, 0:2 * NS],
                            const("own_mask"), ALU.add).then_inc(own_ready, 1)

            for g in range(2):
                with dve.Fori(0, 4) as i:
                    V.loop(i * 8)
                    for j in range(4):
                        for s in range(2, 4):
                            if s == 2:
                                dve.wait_ge(qk_done, i * 4 + (16 * g + j + 1))
                            evacuate(kt_sb[:, j % 2, s].rearrange("p c t -> p (c t)"))
                V.leave(4, 8)

            def choose(g):
                dve.wait_ge(s_evac, 4 * (g + 1) + 1)
                s = s_raw[:, g, :].rearrange("p (b t) -> p b t", b=8)
                w = sm[:, g, :]
                gate, peak, bias = w[:, 0:8], w[:, 8:16], w[:, 24:32]
                v.reduce_sum(gate, s, axis=AXX)
                link(v.reduce_max(peak, s, axis=AXX))
                other = gate.unsqueeze(1).broadcast_to([P, 8, 8])
                this = gate.unsqueeze(2).broadcast_to([P, 8, 8])
                gt, eq = cmp[:, 0], cmp[:, 1]
                v.tensor_tensor(gt, other, this, ALU.is_gt)
                link(v.tensor_tensor(eq, other, this, ALU.is_equal))
                link(v.tensor_tensor(eq, eq, const("before8").rearrange("p (j i) -> p j i", j=8), ALU.mult))
                link(v.tensor_tensor(gt, gt, eq, ALU.add))
                link(v.reduce_sum(w[:, 16:24], gt, axis=AXX))
                link(v.tensor_scalar(bias, w[:, 16:24], 2.5, NEG, ALU.is_gt, ALU.mult))
                link(v.tensor_tensor(peak, peak, bias, ALU.add))
                v.reduce_max(w[:, 34:35], peak, axis=AXX)
                link(v.reduce_max(w[:, 35:36], own_s[:, g, :], axis=AXX))
                link(v.reduce_max(w[:, 33:34], w[:, 34:36], axis=AXX))
                link(v.tensor_scalar(w[:, 32:33], w[:, 33:34], -SCALE, None, ALU.mult))
                v.tensor_scalar(bias, bias, w[:, 32:33], None, ALU.add).then_inc(soft_bias, 1)

            def normalise(g):
                dve.wait_ge(own_probs, g + 1)
                w = sm[:, g, :]
                link(v.reduce_sum(w[:, 49:50], w[:, 40:49], axis=AXX))
                link(v.reciprocal(w[:, 50:51], w[:, 49:50]))
                dve.wait_ge(v_used, 16 * (g + 1))
                v.tensor_scalar(o_sb[g], psum[:, 6 + g, :], w[:, 50:51], None, ALU.mult).then_inc(o_norm, 1)

            def heads_to_mix(g):
                V.wait_full(dve)
                ps = psum[:, V.bank(), :].rearrange("p (c s h i) -> p c s h i", c=4, s=4, h=MH)
                for c in range(4):
                    for u in range(2):
                        dst = mix_t[64 * u:64 * (u + 1), 4 + c, LP + 16 * g:LP + 16 * (g + 1)]
                        ins = v.tensor_copy(dst.rearrange("p (s i) -> p s i", s=4),
                                            ps[64 * u:64 * (u + 1), c, :, 2 * c + u, :])
                V.emptied(ins)

            def evacuate_own(g):
                evacuate(pt_own[0:NS, g, :], rows=NS, width=P)

            choose(0)
            evacuate_block(0)
            evacuate_sample(z[0:NS, 0, 2, :])
            evacuate_own(0)
            causal = const("causal")
            for u in range(6):
                V.wait_full(dve)
                if u < 2:
                    ins = v.tensor_tensor(s_prompt[:, 4 * u:4 * u + 4, :],
                                          psum[:, V.bank(), :].rearrange("p (b t) -> p b t", b=4),
                                          causal.unsqueeze(1).broadcast_to([P, 4, P]), ALU.add)
                else:
                    h = 2 * (u - 2)
                    dst = s_prompt[:, 8 + 2 * h:12 + 2 * h, :].rearrange("p (h b) t -> p h b t", h=2)
                    src = psum[:, V.bank(), :].rearrange("p (h b t) -> p h b t", h=2, b=2)
                    v.tensor_copy(dst[:, :, 0, :], src[:, :, 0, :])
                    ins = v.tensor_tensor(dst[:, :, 1, :], src[:, :, 1, :],
                                          causal.unsqueeze(1).broadcast_to([P, 2, P]), ALU.add)
                n = V.emptied(ins)
            dve.wait_ge(d_empty, n)
            v.reduce_max(pm[:, 0:8], s_prompt[:, 0:8, :], axis=AXX)
            link(v.reduce_max(pm[:, 8:16], s_prompt[:, 8:24, :].rearrange("p (h b) t -> p h (b t)", h=8), axis=AXX))
            v.tensor_scalar(pm[:, 16:32], pm[:, 0:16], -SCALE, None, ALU.mult).then_inc(p_bias, 1)
            dve.wait_ge(mk_stored, 32)
            evacuate_block(1)
            dve.wait_ge(p_exp, 1)
            link(v.reciprocal(pm[:, 48:64], pm[:, 32:48]))
            v.tensor_tensor(s_prompt[:, 0:8, :], s_prompt[:, 0:8, :],
                            pm[:, 48:56].unsqueeze(2).broadcast_to([P, 8, P]), ALU.mult)
            s1 = s_prompt[:, 8:24, :].rearrange("p (h b) t -> p h (b t)", h=8)
            v.tensor_tensor(s1, s1, pm[:, 56:64].unsqueeze(2).broadcast_to([P, 8, LP]), ALU.mult)\
                .then_inc(p_probs, 1)
            for u in range(1, 6, 2):
                evacuate(pt_prompt[:, 4 * u:4 * u + 4, :].rearrange("p b t -> p (b t)"))
            V.wait_full(dve)
            V.emptied(v.tensor_copy(mix_t[:, 6:8, 0:LP],
                                    psum[:, V.bank(), :].rearrange("p (c w) -> p c w", c=2)))
            choose(1)
            dve.wait_ge(mv_stored, 32)
            dve.wait_ge(mvs_ready, 1)
            evacuate_block(2)
            evacuate_sample(z[0:NS, 2, 2, :])
            evacuate_own(1)
            dve.wait_ge(rot_done, 1)
            evacuate_block(0)
            normalise(0)
            heads_to_mix(0)
            evacuate_t(rq_t, 1)
            evacuate_t(rk_t, 1)
            evacuate_t(rk_t, 2)
            dve.wait_ge(qdm_zero, 1)
            V.wait_full(dve)
            V.emptied(v.tensor_copy(
                qdm[:, :, :, 0:4],
                psum[:, V.bank(), 0:P].rearrange("p (h s i) -> p h s i", h=RH, s=SEQS)))
            for tile in range(2):
                V.wait_full(dve)
                V.emptied(v.tensor_tensor(sc_p[:, tile].rearrange("p h t -> p (h t)"), psum[:, V.bank(), :],
                                          const("decay"), ALU.mult))
            V.wait_full(dve)
            V.emptied(v.tensor_tensor(sc_s[0:NS].rearrange("p h t -> p (h t)"), psum[0:NS, V.bank(), 0:P],
                                      const("decay_s")[0:NS], ALU.mult))
            V.wait_full(dve)
            dve.wait_ge(*mark["st1"])
            for h in range(RH):
                ins = v.scalar_tensor_tensor(st2[:, h, :], st1[:, h, :], GAMMA[h] ** P,
                                             psum[:, V.bank(), h * P:(h + 1) * P], ALU.mult, ALU.add)
            dve.wait_ge(d_empty, V.emptied(ins))
            dve.sem_inc(st2_ready, 1)

            def new_states(h):
                for half in range(2):
                    V.wait_full(dve)
                    s = state[:, 4 * half:4 * half + 4, h, :]
                    V.emptied(v.scalar_tensor_tensor(
                        s, s, GAMMA[h] ** 4, psum[:, V.bank(), :].rearrange("p (s d) -> p s d", s=4),
                        ALU.mult, ALU.add))

            dve.wait_ge(state_in, 16)
            new_states(0)
            new_states(1)
            ro, tm = (w.rearrange("p t h d -> p (t h) d") for w in (ret_o, tmp))
            dve.wait_ge(*mark["ret_out"])
            red = pm[:, 0:12]
            link(v.reduce_sum(red, ro, axis=AXX))
            link(v.tensor_scalar(red, red, 1.0 / P, None, ALU.mult))
            link(v.tensor_tensor(ro, ro, red.unsqueeze(2).broadcast_to([P, 12, P]), ALU.subtract))
            link(v.tensor_tensor(tm, ro, ro, ALU.mult))
            link(v.reduce_sum(stat[:, 24:36], tm, axis=AXX))
            dve.sem_inc(var_ready, 1)
            new_states(2)
            dve.wait_ge(sig_ready, 1)
            zg = z[:, 0].rearrange("p t (h d) -> p (t h) d", h=RH)
            sg = sig_g.rearrange("p t h d -> p (t h) d")
            link(v.tensor_tensor(sg, sg, zg, ALU.mult))
            link(v.tensor_tensor(ro, ro, sg, ALU.mult))
            dve.wait_ge(std_ready, 1)
            link(v.reciprocal(red, stat[:, 36:48]))
            v.tensor_tensor(tm, ro, red.unsqueeze(2).broadcast_to([P, 12, P]), ALU.mult)\
                .then_inc(ret_ready, 1)
            new_states(3)
            dve.wait_ge(d_empty, V.n)
            dve.sem_inc(state_new, 1)
            normalise(1)
            evacuate_scaled(mix_t, P, 1, range(4), gain[:, 16:20])
            heads_to_mix(1)
            dve.wait_ge(y_in, 32)
            lo, hi = slice(0, 512), slice(512, D)

            def inverse(n, tile):
                dve.wait_ge(y_std, n + 1)
                v.reciprocal(stat[:, 15 + tile:16 + tile], stat[:, 12 + tile:13 + tile]).then_inc(y_rstd, 1)

            dve.wait_ge(wo_full, 1)
            v.tensor_tensor(y[:, 0, lo], psum[:, 4, :], y[:, 0, lo], ALU.add)
            dve.wait_ge(wo_full, 2)
            v.tensor_tensor(y[:, 0, hi], psum[:, 6, :], y[:, 0, hi], ALU.add).then_inc(y_ready, 1)
            inverse(0, 0)
            dve.wait_ge(*mark["w_out_s0"])
            v.tensor_tensor(y[0:NS, 2, lo], out_s0[0:NS, :], y[0:NS, 2, lo], ALU.add)
            dve.wait_ge(*mark["w_out_s1"])
            v.tensor_tensor(y[0:NS, 2, hi], out_s1[0:NS, :], y[0:NS, 2, hi], ALU.add).then_inc(y_ready, 1)
            inverse(1, 2)
            dve.wait_ge(wo_full, 3)
            v.tensor_tensor(y[:, 1, lo], psum[:, 5, :], y[:, 1, lo], ALU.add)
            dve.wait_ge(st2_stored, 16)
            evacuate_scaled(h2_t, P, 0, range(4, 8), gain[:, 8:16])
            dve.wait_ge(wo_full, 4)
            v.tensor_tensor(y[:, 1, hi], psum[:, 7, :], y[:, 1, hi], ALU.add).then_inc(y_ready, 1)
            inverse(2, 1)
            evacuate_scaled(h2_t, P, 1, range(4, 8), gain[:, 8:16])
            def one_hot(n, slots, first, gated):
                dst = selg if gated else sel
                wide = [P, TILES, 2, SLOTS]
                r = rankm[:, :, bass.ds(first, 2)].unsqueeze(3).broadcast_to(wide)
                i = slots.unsqueeze(1).unsqueeze(1).broadcast_to(wide)
                if not gated:
                    v.tensor_tensor(dst, i, r, ALU.is_equal).then_inc(sel_ready, 1)
                    return
                v.tensor_tensor(dst, i, r, ALU.is_equal).then_inc(selg_eq, 1)
                dve.wait_ge(selg_eq, n + 1)
                w = gates[:, :, bass.ds(first, 2)].unsqueeze(3).broadcast_to(wide)
                v.tensor_tensor(dst, dst, w, ALU.mult).then_inc(selg_ready, 1)

            dve.wait_ge(moe_zero, 1)
            dve.wait_ge(router_in, 32)
            dve.wait_ge(late_in, 16)
            for tile in (0, 2, 1):
                w = COLS[tile]
                dve.wait_ge(lg_full, 2 if tile == 1 else 1)
                link(v.tensor_tensor(lg[0:w, tile, :], psum[0:w, LOGITS[tile], E * tile:E * (tile + 1)], rb[0:w, :],
                                     ALU.add))
                link(v.max(top_v[:, tile, :], lg[:, tile, :]))
                link(v.max_index(top_i[:, tile, :], top_v[:, tile, :], lg[:, tile, :]))
                link(v.tensor_copy(top_f[:, tile, :], top_i[:, tile, 0:4]))
                link(v.tensor_tensor(hot[:, tile], iota[:, 0:E].unsqueeze(1).broadcast_to([P, 4, E]),
                                     top_f[:, tile, :].unsqueeze(2).broadcast_to([P, 4, E]), ALU.is_equal))
                ins = v.reduce_sum(picked[:, tile, :], hot[:, tile].rearrange("p k e -> p e k"), axis=AXX)
                if tile == 2:
                    link(ins)
                    ins = v.tensor_scalar(picked[:, tile, :], picked[:, tile, :],
                                          const("valid")[:, 2:3], None, ALU.mult)
                ins.then_inc(picked_ready, 1)
            v.tensor_tensor(top_w, top_v[:, :, 0:4], top_v[:, :, 0:1].broadcast_to([P, TILES, 4]),
                            ALU.subtract).then_inc(d4_ready, 1)
            dve.wait_ge(picked_ready, 3)
            link(v.tensor_scalar(picked_off, picked, -BIG, BIG, ALU.mult, ALU.add))
            dve.wait_ge(moe_zero, 2)
            dve.wait_ge(rank_full, 1)
            v.tensor_tensor(rankm[:, :, 0:E], psum[:, 5, 0:3 * E].rearrange("p (t e) -> p t e", t=3),
                            picked_off, ALU.add).then_inc(rank_ready, 1)
            slots0 = iota[:, 0:SLOTS]
            dve.wait_ge(rank_ready, 1)
            one_hot(0, slots0, 0, False)
            hot12 = hot.rearrange("p t k e -> p (t k) e")
            hotw12 = hotw.rearrange("p t k e -> p (t k) e")
            valid = const("valid").unsqueeze(2).broadcast_to([P, TILES, E])
            dve.wait_ge(e4_ready, 1)
            link(v.reduce_sum(stat[:, 56:59], top_w, axis=AXX))
            link(v.reciprocal(stat[:, 59:62], stat[:, 56:59]))
            link(v.tensor_tensor(top_w, top_w, stat[:, 59:62].unsqueeze(2).broadcast_to([P, TILES, 4]), ALU.mult))
            link(v.tensor_tensor(hotw12, hot12,
                                 top_w.rearrange("p t k -> p (t k)").unsqueeze(2).broadcast_to([P, 12, E]),
                                 ALU.mult))
            link(v.reduce_sum(gates[:, :, 0:E], hotw.rearrange("p t k e -> p t e k"), axis=AXX))
            v.tensor_tensor(gates[:, :, 0:E], gates[:, :, 0:E], valid, ALU.mult).then_inc(gates_ready, 1)
            dve.wait_ge(rank_full, 2)
            tot = psum[:, 5, 3 * E:4 * E].rearrange("p (n e) -> p n e", e=2)
            link(v.reduce_max(pair_n, tot, axis=AXX))
            flat = flag.rearrange("p r n -> p (r n)")
            link(v.tensor_tensor(flag, pair_n.unsqueeze(1).broadcast_to([P, 4, PAIRS]),
                                 iota[:, SLOTS::SLOTS].unsqueeze(2).broadcast_to([P, 4, PAIRS]), ALU.is_gt))
            link(v.reduce_sum(n_over_f, flat, axis=AXX))
            v.tensor_copy(n_over_i, n_over_f).then_inc(over_ready, 1)

            def choose_bias(first):
                v.tensor_copy(esel, ident[:, bass.ds(first, 2)].unsqueeze(2).broadcast_to([P, 2, SLOTS]))\
                    .then_inc(esel_ready, 1)

            def pair(n, ahead):
                for e in range(2):
                    m = n * 2 + e
                    dve.wait_ge(gu_used, n * 16 + 8 * (e + 1))
                    u = psum[:, 0:2, :].rearrange("p b (f two) -> p b f two", two=2)
                    two = lambda w: w.rearrange("p (b f) -> p b f", b=2)
                    v.tensor_scalar(two(g_sb), u[:, :, :, 0], LIMIT, None, ALU.min).then_inc(glu_ready, 1)
                    v.tensor_scalar(two(l_sb), u[:, :, :, 1], LIMIT, -LIMIT, ALU.min, ALU.max)\
                        .then_inc(u_read, 1)
                    dve.wait_ge(glu_ready, m + 1)
                    dve.wait_ge(u_read, m + 2)
                    v.scalar_tensor_tensor(l_sb, l_sb, 1.0, g_sb, ALU.add, ALU.mult)\
                        .then_inc(lin_ready, 1)
                    dve.wait_ge(lin_ready, m + 1)
                    dve.wait_ge(sigm_ready, m + 1)
                    v.tensor_tensor(a_sb, l_sb, sg_sb, ALU.mult).then_inc(a_ready, 1)
                    if e == 0:
                        added(n)
                    elif ahead:
                        choose_bias(n * 2 + 2)

            def added(n, units=range(6)):
                for i in units:
                    tile, half = i // 2, i % 2
                    w = COLS[tile]
                    dve.wait_ge(comb_full, n * 6 + (i + 1))
                    dst = y[0:w, tile, 512 * half:512 * (half + 1)]
                    v.tensor_tensor(dst, psum[0:w, 3 + half, :], dst, ALU.add).then_inc(comb_added, 1)

            dve.wait_ge(gt_full, 1)
            v.tensor_copy(sgt[0:E, :], psum[0:E, 2, 0:TILES * P]).then_inc(sgt_ready, 1)
            choose_bias(0)
            with dve.Fori(0, PAIRS) as n:
                dve.wait_ge(sgt_full, n + 1)
                one_hot(n, slots0, n * 2, True)
                dve.wait_ge(xt_full, n + 1)
                one_hot(n + 1, slots0, n * 2 + 2, False)
                pair(n, True)
            more = extra_pairs(dve)
            with dve.If(more > 0):
                a, b = before[0:1, 0, :], before[0:1, 1, :]
                f1 = flat[0:1, :]
                link(v.memset(b, 0.0))
                link(v.tensor_copy(b[:, 1:64], f1[:, 0:63]))
                for d in (1, 2, 4, 8, 16, 32):
                    link(v.tensor_copy(a, b))
                    link(v.tensor_tensor(a[:, d:64], b[:, d:64], b[:, 0:64 - d], ALU.add))
                    a, b = b, a
                r1, w1 = round_of[0:1, :], work[0:1]
                link(v.tensor_copy(r1.rearrange("p (r n) -> p r n", r=4),
                                   iota[0:1, SLOTS::SLOTS].unsqueeze(2).broadcast_to([1, 4, PAIRS])))
                link(v.tensor_copy(pair_of[0:1, :].rearrange("p (r n) -> p r n", r=4),
                                   iota[0:1, 0:E:2].unsqueeze(1).broadcast_to([1, 4, PAIRS])))
                for m, what in enumerate((pair_of[0:1, :], r1)):
                    link(v.tensor_tensor(w1, b.unsqueeze(1).broadcast_to([1, EXTRA, 64]),
                                         iota[0:1, 0:EXTRA].unsqueeze(2).broadcast_to([1, EXTRA, 64]),
                                         ALU.is_equal))
                    link(v.tensor_tensor(w1, w1, f1.unsqueeze(1).broadcast_to([1, EXTRA, 64]), ALU.mult))
                    link(v.tensor_tensor(w1, w1, what.unsqueeze(1).broadcast_to([1, EXTRA, 64]), ALU.mult))
                    link(v.reduce_sum(work_f[0:1, m, :], w1, axis=AXX))
                v.tensor_copy(work_i[0:1].rearrange("p a b -> p (a b)"),
                              work_f[0:1].rearrange("p a b -> p (a b)")).then_inc(work_ready, 1)
                dve.wait_ge(work_ready, 1)
                with dve.Fori(PAIRS, more + PAIRS) as n:
                    first = dve.value_load(work_i[0:1, 0, bass.ds(n - PAIRS, 1)], min_val=0, max_val=E - 2)
                    row = dve.value_load(work_i[0:1, 1, bass.ds(n - PAIRS, 1)], min_val=SLOTS,
                                         max_val=(ROUNDS - 1) * SLOTS)
                    slots = iota[:, bass.ds(row, SLOTS)]
                    dve.wait_ge(xt_full, n + 1)
                    one_hot(n + 1, slots, first, False)
                    dve.wait_ge(sgt_full, n + 1)
                    one_hot(n, slots, first, True)
                    choose_bias(first)
                    pair(n, False)
            with dve.Else():
                dve.nop()

            def final_norm(tile):
                w = COLS[tile]
                dve.wait_ge(sq_ready, tile + 1)
                r = stat[:, 53 + tile:54 + tile]
                v.reciprocal(r, r).then_inc(f_rstd, 1)
                dve.wait_ge(f_rstd, tile + 1)
                v.scalar_tensor_tensor(y_out[0:w, tile, :], y[0:w, tile, :], r[0:w], f_gain[0:w, :],
                                       ALU.mult, ALU.mult).then_inc(yo_ready, 1)

            dve.wait_ge(fg_in, 16)
            added(more + PAIRS, range(4))
            final_norm(0)
            added(more + PAIRS, range(4, 6))
            final_norm(1)
            final_norm(2)

        @block.gpsimd
        def _(pool):
            g_ = nc.gpsimd
            chain = [0]

            def link(ins):
                chain[0] += 1
                ins.then_inc(pool_step, 1)
                pool.wait_ge(pool_step, chain[0])

            link(g_.memset(stat, 0.0))
            pool.sem_inc(zeroed, 1)
            link(g_.memset(z.rearrange("p a b c -> p (a b c)"), 0.0))
            pool.sem_inc(zeroed, 1)
            link(g_.memset(q_blk.rearrange("p a b c -> p (a b c)"), 0.0))
            pool.wait_ge(pages_in, 16)
            load_pages(pool, POOL_SEQS, kv_pool_in, ck, 0, 0, lambda j: None)
            wait_all(pool, mark["mq_t"])
            for c in range(4):
                for u in range(2):
                    h = 2 * c + u
                    ins = g_.tensor_copy(q_blk[64 * u:64 * (u + 1), :, c, 4 * h:4 * h + 4],
                                         mq_t[64 * u:64 * (u + 1), c, LP:TOK].rearrange("p (s i) -> p s i", s=SEQS))
            ins.then_inc(qblk_ready, 1)
            def store(prompt, sampled, slot, done):
                pool.dma_start(prompt[0, 0].rearrange("(t p) h d -> p t (h d)", p=P),
                               z[:, slot, 0:2, :]).then_inc(done, 16)
                pool.dma_start(sampled[0].rearrange("s i h d -> (s i) (h d)"),
                               z[0:NS, slot, 2, :]).then_inc(done, 16)

            wait_all(pool, mark["z1"])
            store(outs[2], outs[5], 1, mk_stored)
            wait_all(pool, mark["z2"])
            g_.tensor_copy(mv_s[0:NS, :], z[0:NS, 2, 2, :]).then_inc(mvs_ready, 1)
            store(outs[3], outs[6], 2, mv_stored)
            for i in range(1, 4):
                k_pages(pool, POOL_SEQS, kv_pool_in, 0, i)
            with pool.Fori(0, 4) as i:
                k_pages(pool, POOL_SEQS, kv_pool_in, 1, i)
            cos, sin = (const(n).rearrange("p (t f) -> p t f", t=TILES).unsqueeze(2)
                        .broadcast_to([P, TILES, RH, 64]) for n in ("cos", "sin"))
            pool.wait_ge(tables_in, 16)
            wait_all(pool, mark["prompt_o"])
            t1, t2 = tmp[:, :, :, 0:64], tmp[:, :, :, 64:128]
            for slot, dst, waits in ((0, rot_q, mark["z3"]), (1, rot_k, mark["z4"])):
                wait_all(pool, waits)
                src = z[:, slot].rearrange("p t (h d) -> p t h d", h=RH)
                x1, x2 = src[:, :, :, 0:64], src[:, :, :, 64:128]
                o1, o2 = dst[:, :, :, 0:64], dst[:, :, :, 64:128]
                g_.tensor_tensor(t1, x2, sin, ALU.mult)
                g_.tensor_tensor(o1, x1, cos, ALU.mult)
                g_.tensor_tensor(t2, x1, sin, ALU.mult)
                link(g_.tensor_tensor(o2, x2, cos, ALU.mult))
                g_.tensor_tensor(o1, o1, t1, ALU.subtract)
                link(g_.tensor_tensor(o2, o2, t2, ALU.add))
                pool.sem_inc(rot_done, 1)
            qd = const("q_dec").rearrange("p (t h) -> p t h", t=TILES)
            kd = const("k_dec").rearrange("p (t h) -> p t h", t=TILES)
            g_.tensor_tensor(q_dec, rot_q[:, 1:3], qd[:, 1:3].unsqueeze(3).broadcast_to([P, 2, RH, P]),
                             ALU.mult).then_inc(qdec_ready, 1)
            g_.tensor_tensor(k_dec, rot_k, kd.unsqueeze(3).broadcast_to([P, TILES, RH, P]),
                             ALU.mult).then_inc(kdec_ready, 1)
            pool.wait_ge(*mark["block6"])
            link(g_.memset(qdm_flat.rearrange("p a b -> p (a b)"), 0.0))
            pool.sem_inc(qdm_zero, 1)
            pool.wait_ge(*mark["pt3"])
            wait_all(pool, mark["z5"])
            for h in range(RH):
                if h:
                    pool.wait_ge(*mark[f"vblk{h - 1}"])
                g_.tensor_tensor(v_blk[0:NS],
                                 z[0:NS, 2, 2, h * P:(h + 1) * P].unsqueeze(1).broadcast_to([NS, SEQS, P]),
                                 const("seq_mask")[0:NS].unsqueeze(2).broadcast_to([NS, SEQS, P]),
                                 ALU.mult).then_inc(vblk_ready, 1)
            pool.wait_ge(st2_ready, 1)
            pool.dma_start(outs[4][0, 0].rearrange("h k v -> k h v"), st2).then_inc(st2_stored, 16)
            pool.wait_ge(state_new, 1)
            pool.dma_start(outs[7][0].rearrange("s h k v -> k (s h) v"),
                           state.rearrange("p s h v -> p (s h) v")).then_inc(state_stored, 16)
            pool.wait_ge(*mark["pt7"])
            link(g_.memset(y[:, 2, :], 0.0))
            pool.sem_inc(y_zero, 1)
            wait_all(pool, mark["ret_mix"])
            link(g_.memset(lg.rearrange("p a b -> p (a b)"), 0.0))
            g_.memset(bgu, 0.0)
            g_.memset(sgt, 0.0)
            link(g_.memset(out2, 0.0))
            pool.sem_inc(moe_zero, 1)
            pool.wait_ge(*mark["w_out"])
            g_.memset(rankm.rearrange("p a b -> p (a b)"), BIG)
            link(g_.memset(gates.rearrange("p a b -> p (a b)"), 0.0))
            pool.sem_inc(moe_zero, 1)

        @block.sync
        def _(sp):
            head = table["eps"][0] + 1
            sp.dma_start(consts[:, 0:head], t["shape_consts"][:, 0:head]).then_inc(consts_in, 16)
            sp.dma_start(x_sb[0:NS, 2, :], x_s).then_inc(x_in[2], 16)
            sp.dma_start(x_sb[:, 0, :], x_p[:, 0, :]).then_inc(x_in[0], 16)
            sp.dma_start(gain_in[0:8, :], t["norm1_g"][0].rearrange("(k p) -> k p", p=P)).then_inc(gains_in, 16)
            sp.dma_start(gain_in[8:16, :], t["norm2_g"][0].rearrange("(k p) -> k p", p=P)).then_inc(gains_in, 16)
            sp.dma_start(gain_in[16:20, :], t["ret_norm_g"][0].rearrange("(k p) -> k p", p=P)).then_inc(gains_in, 16)
            sp.dma_start(x_sb[:, 1, :], x_p[:, 1, :]).then_inc(x_in[1], 16)

            def load_block(b):
                if b >= 3:
                    sp.wait_ge(*mark[f"block{b - 3}"])
                src = w_in[:, :, 512 * BLOCKS[b]:512 * (BLOCKS[b] + 1)] if b < 7 else \
                    w_out[:, :, 512 * (b - 7):512 * (b - 6)]
                sp.dma_start(win[:, b % 3], src).then_inc(win_in[b % 3], 16)

            load_block(0)
            sp.dma_start(page_sb[:, :], t["page_table"].rearrange("(a s) n -> a (s n)", a=1)).then_inc(pages_in, 16)
            load_block(1)
            sp.dma_start(consts[:, head:], t["shape_consts"][:, head:ncols]).then_inc(tables_in, 16)
            sp.wait_ge(pages_in, 16)
            load_pages(sp, SP_SEQS, kv_in, ck, 0, 0, lambda j: None)
            load_block(2)
            load_block(3)
            load_block(4)
            k_pages(sp, SP_SEQS, kv_in, 0, 1)
            k_pages(sp, SP_SEQS, kv_in, 0, 2)
            k_pages(sp, SP_SEQS, kv_in, 0, 3)
            with sp.Fori(0, 4) as i:
                k_pages(sp, SP_SEQS, kv_in, 1, i)
            for v in range(8):
                def wait(j, v=v):
                    if v == 0:
                        sp.wait_ge(d_full, mark["k_base"] + 64 + 2 * j - 6)
                    else:
                        sp.wait_ge(v_used, 4 * (v - 1) + j + 1)
                load_pages(sp, range(4), kv_in, cv, v // 4, v % 4, wait)
                if v == 0:
                    load_block(5)
                    load_block(6)
                if v == 2:
                    load_block(7)
                if v == 3:
                    sp.dma_start(state.rearrange("p s h v -> p (s h) v"),
                                 t["state_ret"][0].rearrange("s h k v -> k (s h) v")).then_inc(state_in, 16)
                if v == 4:
                    load_block(8)

            def load_gu(e, k, one=0):
                src = w_gu[e] if isinstance(e, int) else w_gu[bass.ds(e, 1)].rearrange("a d f -> (a d) f")
                src = src[P * k:P * (k + 1), :]
                if one and k < AHEAD:
                    sp.dma_start(gu_odd[k], src).then_inc(gu_odd_in[k], 16)
                else:
                    sp.dma_start(gu[:, k, :], src).then_inc(gu_in[k], 16)

            def load_dn(e, q):
                src = w_dn[e] if isinstance(e, int) else w_dn[bass.ds(e, 1)].rearrange("a d f -> (a d) f")
                sp.dma_start(dn[:, 2 * q:2 * q + 2, :],
                             src[2 * P * q:2 * P * (q + 1), :].rearrange("(m p) n -> p m n", p=P))\
                    .then_inc(dn_in[q], 16)

            sp.wait_ge(*mark["block6"])
            load_gu(0, 0)
            load_gu(0, 1)
            sp.wait_ge(rot_done, 2)
            sp.dma_start(rw, t["router_w"][0].rearrange("(k p) e -> p k e", p=P)).then_inc(router_in, 16)
            sp.dma_start(rb, t["router_b"][0:1].partition_broadcast(P).rearrange("p a e -> p (a e)"))\
                .then_inc(router_in, 16)
            sp.wait_ge(*mark["pt7"])
            sp.wait_ge(y_zero, 1)
            sp.dma_start(y[:, 0:2, :], x_p).then_inc(y_in, 16)
            sp.dma_start(y[0:NS, 2, :], x_s).then_inc(y_in, 16)
            sp.dma_start(f_gain, t["final_norm_g"].partition_broadcast(P)).then_inc(fg_in, 16)
            sp.wait_ge(moe_zero, 1)
            sp.dma_start(bgu[0:E, :], t["b_gate_up"][0]).then_inc(bias_in, 16)
            sp.dma_start(out2[0:E, :], t["b_down"][0]).then_inc(bias_in, 16)
            sp.wait_ge(st2_ready, 1)
            sp.dma_start(late, t["shape_consts"][:, ncols:ncols + late_cols]).then_inc(late_in, 16)
            sp.wait_ge(state_stored, 16)
            load_gu(0, 6)
            load_gu(0, 7)
            sp.wait_ge(ret_ready, 1)
            for q in range(4):
                load_dn(0, q)
            sp.wait_ge(*mark["w_out"])
            for k in range(2, 6):
                load_gu(0, k)

            def load_gate_up(e, n, one, chunks):
                for k in chunks:
                    sp.wait_ge(gu_used, n * 16 + (8 * one + k - (15 if k < AHEAD else 7)))
                    load_gu(e, k, one)

            def load_down(e, n, one):
                for q in range(4):
                    sp.wait_ge(dn_used, n * 8 + (4 * one + q - 3))
                    load_dn(e, q)

            first, others = range(AHEAD), range(AHEAD, KC)
            load_gu(1, 0, 1)
            sp.wait_ge(lg_full, 2)
            load_gu(1, 1, 1)
            load_gate_up(1, 0, 1, others)
            load_gate_up(2, 1, 0, first)
            load_down(1, 0, 1)

            def load_pair(e, n, following):
                load_gate_up(e, n, 0, others)
                load_gate_up(e + 1, n, 1, first)
                load_down(e, n, 0)
                load_gate_up(e + 1, n, 1, others)
                if following:
                    load_gate_up(e + 2, n + 1, 0, first)
                load_down(e + 1, n, 1)

            with sp.Fori(1, PAIRS - 1) as n:
                load_pair(n * 2, n, True)
            load_pair(E - 2, PAIRS - 1, False)
            more = extra_pairs(sp)
            with sp.If(more > 0):
                sp.wait_ge(work_ready, 1)
                with sp.Fori(PAIRS, more + PAIRS) as n:
                    e = sp.value_load(work_i[0:1, 0, bass.ds(n - PAIRS, 1)], min_val=0, max_val=E - 2)
                    load_gate_up(e, n, 0, first)
                    load_pair(e, n, False)
            with sp.Else():
                sp.nop()
            for tile in range(2):
                sp.wait_ge(yo_ready, tile + 1)
                sp.dma_start(outs[0][0].rearrange("(t p) d -> p t d", p=P)[:, tile, :], y_out[:, tile, :])\
                    .then_inc(stored, 16)
            sp.wait_ge(yo_ready, 3)
            sp.dma_start(outs[1].rearrange("s i d -> (s i) d"), y_out[0:NS, 2, :]).then_inc(stored, 16)
            sp.wait_ge(stored, 48)
            sp.wait_ge(st2_stored, 16)
            sp.wait_ge(mk_stored, 32)
            sp.wait_ge(mv_stored, 32)
            sp.wait_ge(state_stored, 16)


_INS = ["x_prompt", "x_sample", "cache_k", "cache_v", "state_ret", "page_table", "norm1_g", "w_in",
        "ret_norm_g", "w_out", "norm2_g", "router_w", "router_b", "w_gate_up", "b_gate_up",
        "w_down", "b_down", "final_norm_g"]
_OUTS = [(1, 256, 1024), (8, 4, 1024), (1, 1, 256, 8, 64), (1, 1, 256, 8, 64), (1, 1, 4, 128, 128),
         (1, 8, 4, 8, 64), (1, 8, 4, 8, 64), (1, 8, 4, 128, 128)]


def kernel(**inputs):
    import concourse.bacc as _bacc
    from concourse.bass_utils import run_bass_kernel_spmd as _run

    nc = _bacc.Bacc("TRN2", target_bir_lowering=False, num_devices=1)
    arrays = {name: np.ascontiguousarray(inputs[name]) for name in _INS}
    table, arrays["shape_consts"] = shape_constants()
    tensors = {name: nc.dram_tensor(name, a.shape, mybir.dt.from_np(a.dtype), kind="ExternalInput").ap()
               for name, a in arrays.items()}
    outs = [nc.dram_tensor(f"out_{i}", shape, F32, kind="ExternalOutput").ap()
            for i, shape in enumerate(_OUTS)]
    build_kernel(nc, tensors, table, outs)
    r = _run(nc, [arrays], core_ids=[0])
    return tuple(r.results[0][f"out_{i}"] for i in range(len(_OUTS)))
```
